# Optimizing a Trainium2 kernel written in Bass

```python
import math
import jax, jax.numpy as jnp
from jax import lax
import numpy as np

D_MODEL = 1024
BATCH = 1
SEQ = 256
DEPTH = 1

CTX_LEN = 256
GRID_W = 64
EPS = 1e-6

HG_HEADS = 4
HG_DK = 128
HG_DV = 128
HG_KDIM = HG_HEADS * HG_DK
HG_WIDTH = HG_HEADS * HG_DV
CHUNK = 32

HY_WIDTH = 512
HY_SHORT = 3
HY_EMB = 33
HY_FILTER_HIDDEN = 64
HY_FILTER_SCALE = 0.05
HY_DECAY_TARGET = 1e-2
HY_FAST_PCT = 0.3
HY_SLOW_PCT = 1.5

SPLIT_POINTS = (HG_KDIM, 2 * HG_KDIM, 3 * HG_KDIM, 3 * HG_KDIM + HG_WIDTH,
                3 * HG_KDIM + 2 * HG_WIDTH, 3 * HG_KDIM + 2 * HG_WIDTH + 3 * HY_WIDTH)
IN_WIDTH = 3 * HG_KDIM + 2 * HG_WIDTH + 3 * HY_WIDTH + 2 * D_MODEL

N_GROUPS = 4
EXPERTS_PER_GROUP = 8
TOP_K = 2
D_EXPERT = 512


F32 = jnp.float32

def rms_norm(x, g):
    xf = x.astype(F32)
    y = xf * lax.rsqrt(jnp.mean(xf * xf, axis=-1, keepdims=True) + EPS)
    return (y * g.astype(F32)).astype(x.dtype)

def adaln(cvec, w, b):
    m = jax.nn.silu(cvec) @ w + b
    return [t[..., None, :] for t in jnp.split(m, 6, axis=-1)]

def modulate(h, shift, scale):
    return h * (1.0 + scale) + shift

def sincos_2d(n_tokens):
    rows = n_tokens // GRID_W
    r = jnp.repeat(jnp.arange(rows, dtype=F32), GRID_W)
    col = jnp.tile(jnp.arange(GRID_W, dtype=F32), rows)
    quarter = D_MODEL // 4
    omega = 1.0 / (10000.0 ** (jnp.arange(quarter, dtype=F32) / quarter))

    def axis_emb(pos):
        a = pos[:, None] * omega[None, :]
        return jnp.concatenate([jnp.sin(a), jnp.cos(a)], axis=-1)

    return jnp.concatenate([axis_emb(r), axis_emb(col)], axis=-1)

def lower_bounds(lb_param):
    p = jax.nn.softmax(lb_param.astype(F32), axis=0)
    return jnp.cumsum(p, axis=0)[:DEPTH]

def heads(t, d):
    B, L, _ = t.shape
    return t.reshape(B, L, HG_HEADS, d).transpose(0, 2, 1, 3)

def flip(t):
    return jnp.flip(t, axis=2)

def hgrn2_keys(z, lb):
    z = z.astype(F32)
    log_f = jnp.log(lb + (1.0 - lb) * jax.nn.sigmoid(z))
    k = (1.0 - lb) * jax.nn.sigmoid(-z)
    return heads(k, HG_DK), heads(log_f, HG_DK)

def gla_chunk_scan(q, k, v, log_f, s0):
    B, H, L, DK = q.shape
    DV = v.shape[-1]
    n = L // CHUNK

    def to_chunks(t):
        return t.reshape(B, H, n, CHUNK, t.shape[-1]).transpose(2, 0, 1, 3, 4)

    b = to_chunks(lax.cumsum(log_f.reshape(B, H, n, CHUNK, DK), axis=3).reshape(B, H, L, DK))
    mask = jnp.tril(jnp.ones((CHUNK, CHUNK), dtype=bool))
    mid = CHUNK // 2

    def step(S, xs):
        qc, kc, vc, bc = xs
        total = bc[:, :, -1:, :]
        ref = bc[:, :, mid:mid + 1, :]
        scores = jnp.einsum('bhtk,bhsk->bhts', qc * jnp.exp(bc - ref), kc * jnp.exp(ref - bc))
        scores = jnp.where(mask, scores, 0.0)
        o = (jnp.einsum('bhtk,bhkv->bhtv', qc * jnp.exp(bc), S)
             + jnp.einsum('bhts,bhsv->bhtv', scores, vc))
        S_new = (jnp.exp(total[:, :, 0, :])[..., None] * S
                 + jnp.einsum('bhsk,bhsv->bhkv', kc * jnp.exp(total - bc), vc))
        return S_new, o

    s_fin, o = lax.scan(step, s0, (to_chunks(q), to_chunks(k), to_chunks(v), b))
    return o.transpose(1, 2, 0, 3, 4).reshape(B, H, L, DV), s_fin

def gla_final_state(k, v, log_f):
    decay = jnp.exp(lax.cumsum(log_f, axis=2, reverse=True) - log_f)
    return jnp.einsum('bhlk,bhlv->bhkv', k * decay, v)

def hgrn2_bidir(q, v, fwd, bwd, s0_f, s0_b):
    o_f, s_f = gla_chunk_scan(q, fwd[0], v, fwd[1], s0_f)
    o_b, s_b = gla_chunk_scan(flip(q), flip(bwd[0]), flip(v), flip(bwd[1]), s0_b)
    return o_f + flip(o_b), s_f, s_b

def hgrn2_readout(o, g, norm_g, dtype):
    o = o * lax.rsqrt(jnp.mean(o * o, axis=-1, keepdims=True) + EPS) * norm_g.astype(F32)
    B, H, L, DV = o.shape
    o = o.transpose(0, 2, 1, 3).reshape(B, L, H * DV)
    return (o * jax.nn.silu(g.astype(F32))).astype(dtype)

def short_conv3(u, w, b):
    up = jnp.pad(u, ((0, 0), (1, 1), (0, 0)))
    return up[:, :-2] * w[0] + up[:, 1:-1] * w[1] + up[:, 2:] * w[2] + b

def hyena_filters(L, w1, b1, fr1, w2, b2, fr2, w3):
    t = jnp.linspace(0.0, 1.0, L, dtype=F32)[:, None]
    bands = (HY_EMB - 1) // 2
    ang = (2.0 * math.pi * jnp.arange(L, dtype=F32) / L)[:, None] * \
        jnp.linspace(1e-4, bands - 1, bands, dtype=F32)[None, :]
    z = jnp.concatenate([t, jnp.cos(ang), -jnp.sin(ang)], axis=-1)
    h = jnp.sin(fr1.astype(F32) * (z @ w1.astype(F32) + b1.astype(F32)))
    h = jnp.sin(fr2.astype(F32) * (h @ w2.astype(F32) + b2.astype(F32)))
    h = h @ w3.astype(F32)
    deltas = jnp.abs(jnp.linspace(math.log(HY_DECAY_TARGET) / HY_SLOW_PCT,
                                  math.log(HY_DECAY_TARGET) / HY_FAST_PCT, HY_WIDTH, dtype=F32))
    h = h.reshape(L, 2, HY_WIDTH) * jnp.exp(-t * deltas)[:, None, :]
    return h[:, 0], h[:, 1]

def long_conv_bidir(u, h_fwd, h_bwd, d_skip):
    B, L, C = u.shape
    kern = jnp.concatenate([h_fwd, jnp.zeros((1, C), F32), jnp.flip(h_bwd[1:], axis=0)], axis=0)
    y = jnp.fft.irfft(jnp.fft.rfft(u, n=2 * L, axis=1) * jnp.fft.rfft(kern, axis=0)[None],
                      n=2 * L, axis=1)[:, :L]
    return y + u * d_skip

def hyena_branch(p_hy, conv_w, conv_b, filt, d_skip):
    L = p_hy.shape[1]
    u = short_conv3(p_hy, conv_w, conv_b).astype(F32)
    v, x1, x0 = jnp.split(u, 3, axis=-1)
    h_fwd, h_bwd = hyena_filters(L, *filt)
    y = x0 * long_conv_bidir(v * x1, h_fwd, h_bwd, d_skip.astype(F32))
    return y.astype(p_hy.dtype)

def merge_branches(y_a, y_b, g_logits, w_pa, w_pb, w_o):
    g_a, g_b = jnp.split(g_logits, 2, axis=-1)
    mixed = jax.nn.sigmoid(g_a) * (y_a @ w_pa) + jax.nn.sigmoid(g_b) * (y_b @ w_pb)
    return mixed @ w_o

def token_mixer(p, lb, s0_f, s0_b, hg_norm_g, conv_w, conv_b, filt, d_skip, w_pa, w_pb, w_o):
    q, z_f, z_b, vi, g, p_hy, g_logits = jnp.split(p, SPLIT_POINTS, axis=-1)
    fwd = hgrn2_keys(z_f, lb[0])
    bwd = hgrn2_keys(z_b, lb[1])
    o, s_f, s_b = hgrn2_bidir(heads(q.astype(F32), HG_DK), heads(vi.astype(F32), HG_DV),
                              fwd, bwd, s0_f, s0_b)
    y_a = hgrn2_readout(o, g, hg_norm_g, p.dtype)
    y_b = hyena_branch(p_hy, conv_w, conv_b, filt, d_skip)
    return merge_branches(y_a, y_b, g_logits, w_pa, w_pb, w_o), s_f, s_b

def context_states(p_c, lb):
    z_f, z_b, vi = jnp.split(p_c, (HG_KDIM, 2 * HG_KDIM), axis=-1)
    kf, lf = hgrn2_keys(z_f, lb[0])
    kb, lb_ = hgrn2_keys(z_b, lb[1])
    v = heads(vi.astype(F32), HG_DV)
    return gla_final_state(kf, v, lf), gla_final_state(flip(kb), flip(v), flip(lb_))

def hier_moe(h, wg, bg, we, be, w_gate, w_up, w_down):
    B, L, D = h.shape
    t = h.reshape(B * L, D)
    p_group = jax.nn.softmax((t @ wg + bg).astype(F32), axis=-1)
    p_top_g, g_idx = lax.top_k(p_group, 1)
    e_logits = (jnp.einsum('td,gde->tge', t, we) + be).astype(F32)
    e_logits = jnp.take_along_axis(e_logits, g_idx[:, :, None], axis=1)[:, 0]
    p_top_e, e_idx = lax.top_k(jax.nn.softmax(e_logits, axis=-1), TOP_K)
    w_sel = p_top_g * p_top_e / jnp.sum(p_top_e, axis=-1, keepdims=True)
    combine = (jnp.einsum('tk,tke->te', w_sel, jax.nn.one_hot(e_idx, EXPERTS_PER_GROUP, dtype=F32))[:, None, :]
               * jax.nn.one_hot(g_idx[:, 0], N_GROUPS, dtype=F32)[:, :, None])
    out = jnp.zeros((B * L, D), F32)
    for gi in range(N_GROUPS):
        hid = (jax.nn.silu(jnp.einsum('td,edf->tef', t, w_gate[gi]))
               * jnp.einsum('td,edf->tef', t, w_up[gi])
               * combine[:, gi, :, None].astype(t.dtype))
        out = out + jnp.einsum('tef,efd->td', hid, w_down[gi])
    return out.reshape(B, L, D).astype(h.dtype)

def first_inputs(seed: int = 0) -> dict:
    key = jax.random.key(seed)
    ks = jax.random.split(key, 32)

    def nrm(k, shape, scale):
        return scale * jax.random.normal(k, shape, F32)

    G, E, F = N_GROUPS, EXPERTS_PER_GROUP, D_EXPERT
    return {
        "x": nrm(ks[0], (BATCH, SEQ, D_MODEL), 1.0),
        "c": nrm(ks[1], (BATCH, D_MODEL), 1.0),
        "ctx": nrm(ks[2], (BATCH, CTX_LEN, D_MODEL), 1.0),
        "c_ctx": nrm(ks[3], (D_MODEL,), 1.0),
        "ada_w": nrm(ks[4], (DEPTH, D_MODEL, 6 * D_MODEL), 0.5 * D_MODEL ** -0.5),
        "ada_b": nrm(ks[5], (DEPTH, 6 * D_MODEL), 0.02),
        "norm1_g": 1.0 + nrm(ks[6], (DEPTH, D_MODEL), 0.05),
        "norm2_g": 1.0 + nrm(ks[7], (DEPTH, D_MODEL), 0.05),
        "w_in": nrm(ks[8], (DEPTH, D_MODEL, IN_WIDTH), D_MODEL ** -0.5),
        "hgrn_lb": nrm(ks[9], (DEPTH + 1, 2, HG_KDIM), 0.1),
        "hgrn_norm_g": 1.0 + nrm(ks[10], (DEPTH, HG_DV), 0.05),
        "hy_conv_w": nrm(ks[11], (DEPTH, HY_SHORT, 3 * HY_WIDTH), HY_SHORT ** -0.5),
        "hy_conv_b": nrm(ks[12], (DEPTH, 3 * HY_WIDTH), 0.02),
        "hy_filt_w1": nrm(ks[13], (DEPTH, HY_EMB, HY_FILTER_HIDDEN), HY_EMB ** -0.5),
        "hy_filt_b1": nrm(ks[14], (DEPTH, HY_FILTER_HIDDEN), 0.1),
        "hy_filt_freq1": 1.0 + nrm(ks[15], (DEPTH, HY_FILTER_HIDDEN), 0.1),
        "hy_filt_w2": nrm(ks[16], (DEPTH, HY_FILTER_HIDDEN, HY_FILTER_HIDDEN), HY_FILTER_HIDDEN ** -0.5),
        "hy_filt_b2": nrm(ks[17], (DEPTH, HY_FILTER_HIDDEN), 0.1),
        "hy_filt_freq2": 1.0 + nrm(ks[18], (DEPTH, HY_FILTER_HIDDEN), 0.1),
        "hy_filt_w3": nrm(ks[19], (DEPTH, HY_FILTER_HIDDEN, 2 * HY_WIDTH), HY_FILTER_SCALE * HY_FILTER_HIDDEN ** -0.5),
        "hy_d": nrm(ks[20], (DEPTH, HY_WIDTH), 0.1),
        "w_proj_a": nrm(ks[21], (DEPTH, HG_WIDTH, D_MODEL), HG_WIDTH ** -0.5),
        "w_proj_b": nrm(ks[22], (DEPTH, HY_WIDTH, D_MODEL), HY_WIDTH ** -0.5),
        "w_out": nrm(ks[23], (DEPTH, D_MODEL, D_MODEL), D_MODEL ** -0.5),
        "moe_router_g_w": nrm(ks[24], (DEPTH, D_MODEL, G), D_MODEL ** -0.5),
        "moe_router_g_b": nrm(ks[25], (DEPTH, G), 0.01),
        "moe_router_e_w": nrm(ks[26], (DEPTH, G, D_MODEL, E), D_MODEL ** -0.5),
        "moe_router_e_b": nrm(ks[27], (DEPTH, G, E), 0.01),
        "moe_w_gate": nrm(ks[28], (DEPTH, G, E, D_MODEL, F), D_MODEL ** -0.5),
        "moe_w_up": nrm(ks[29], (DEPTH, G, E, D_MODEL, F), D_MODEL ** -0.5),
        "moe_w_down": nrm(ks[30], (DEPTH, G, E, F, D_MODEL), F ** -0.5),
        "final_norm_g": 1.0 + nrm(ks[31], (D_MODEL,), 0.05),
    }

def first_block(x, c, ctx, c_ctx, ada_w, ada_b, norm1_g, norm2_g, w_in, hgrn_lb, hgrn_norm_g,
              hy_conv_w, hy_conv_b, hy_filt_w1, hy_filt_b1, hy_filt_freq1, hy_filt_w2, hy_filt_b2,
              hy_filt_freq2, hy_filt_w3, hy_d, w_proj_a, w_proj_b, w_out, moe_router_g_w,
              moe_router_g_b, moe_router_e_w, moe_router_e_b, moe_w_gate, moe_w_up, moe_w_down,
              final_norm_g):
    B = x.shape[0]
    x = x + sincos_2d(x.shape[1]).astype(x.dtype)
    lbs = lower_bounds(hgrn_lb)
    zero_state = jnp.zeros((B, HG_HEADS, HG_DK, HG_DV), F32)
    for l in range(DEPTH):
        last = l == DEPTH - 1
        sh1, sc1, gt1, sh2, sc2, gt2 = adaln(c, ada_w[l], ada_b[l])
        csh1, csc1, cgt1, csh2, csc2, cgt2 = adaln(c_ctx, ada_w[l], ada_b[l])
        filt = (hy_filt_w1[l], hy_filt_b1[l], hy_filt_freq1[l], hy_filt_w2[l], hy_filt_b2[l],
                hy_filt_freq2[l], hy_filt_w3[l])
        mix_args = (hgrn_norm_g[l], hy_conv_w[l], hy_conv_b[l], filt, hy_d[l],
                    w_proj_a[l], w_proj_b[l], w_out[l])
        hc = modulate(rms_norm(ctx, norm1_g[l]), csh1, csc1)
        if last:
            s_f, s_b = context_states(hc @ w_in[l][:, HG_KDIM:3 * HG_KDIM + HG_WIDTH], lbs[l])
        else:
            ctx_mix, s_f, s_b = token_mixer(hc @ w_in[l], lbs[l], zero_state, zero_state, *mix_args)
        hx = modulate(rms_norm(x, norm1_g[l]), sh1, sc1)
        x_mix, _, _ = token_mixer(hx @ w_in[l], lbs[l], s_f, s_b, *mix_args)
        x = x + gt1 * x_mix
        moe_args = (moe_router_g_w[l], moe_router_g_b[l], moe_router_e_w[l], moe_router_e_b[l],
                    moe_w_gate[l], moe_w_up[l], moe_w_down[l])
        x = x + gt2 * hier_moe(modulate(rms_norm(x, norm2_g[l]), sh2, sc2), *moe_args)
        if not last:
            ctx = ctx + cgt1 * ctx_mix
            ctx = ctx + cgt2 * hier_moe(modulate(rms_norm(ctx, norm2_g[l]), csh2, csc2), *moe_args)
    return rms_norm(x, final_norm_g)


DEPTH_2 = 2

N_EVEN = (DEPTH_2 + 1) // 2
N_ODD = DEPTH_2 // 2

M_HEADS = 4
M_HEAD_DIM = D_MODEL // M_HEADS
M_WIDTH = M_HEADS * M_HEAD_DIM
M_CHUNK = 128
M_CONV = 3
P_WINDOWS = (2, 4, 8, 16)
P_GROUPS = len(P_WINDOWS)
P_GROUP_DIM = D_MODEL // P_GROUPS
P_WIDTH = P_GROUPS * P_GROUP_DIM
AB_WIDTH = M_WIDTH + P_WIDTH
N_GATE = 4 * M_HEADS
GATE_OFF = 5 * M_WIDTH + 2 * P_WIDTH
AB_IN = GATE_OFF + N_GATE

A_HEADS = 16
A_KV_HEADS = 4
A_GROUP = A_HEADS // A_KV_HEADS
A_HEAD_DIM = D_MODEL // A_HEADS
A_WIDTH = A_HEADS * A_HEAD_DIM
A_KV_WIDTH = A_KV_HEADS * A_HEAD_DIM
A_WINDOW = 128
A_BLOCK = 128
A_BAND = A_BLOCK + 2 * A_WINDOW
ROPE_BASE = 10000.0
C_IN = 2 * A_WIDTH + 2 * A_KV_WIDTH


f32 = jnp.float32

def rmsnorm(x, g):
    xf = x.astype(f32)
    return (xf * lax.rsqrt(jnp.mean(xf * xf, -1, keepdims=True) + EPS) * g).astype(x.dtype)

def short_conv(u, w):
    pad = w.shape[0] // 2
    return lax.conv_general_dilated(u, w[:, None, :].astype(u.dtype), (1,), [(pad, pad)],
                                    dimension_numbers=('NWC', 'WIO', 'NWC'),
                                    feature_group_count=u.shape[-1])

def to_heads(a):
    bsz, n, _ = a.shape
    return a.reshape(bsz, n, M_HEADS, M_HEAD_DIM).transpose(0, 2, 1, 3).astype(f32)

def mlstm_chunkwise(q, k, v, log_i, log_f, state):
    bsz, nh, n, dh = q.shape
    nc = n // M_CHUNK

    def chunks(a):
        return jnp.moveaxis(a.reshape(a.shape[:2] + (nc, M_CHUNK) + a.shape[3:]), 2, 0)

    lower = jnp.tril(jnp.ones((M_CHUNK, M_CHUNK), bool))

    def step(carry, inp):
        c_mem, n_mem, m_prev = carry
        qc, kc, vc, lic, lfc = inp
        b = jnp.cumsum(lfc, axis=-1)
        dmat = b[..., :, None] - b[..., None, :] + lic[..., None, :]
        dmat = jnp.where(lower, dmat, -jnp.inf)
        inter = b + m_prev[..., None]
        m_t = jnp.maximum(inter, dmat.max(-1))
        w_inter = jnp.exp(inter - m_t)
        s = jnp.einsum('bhtd,bhsd->bhts', qc, kc) * jnp.exp(dmat - m_t[..., None])
        num = w_inter[..., None] * jnp.einsum('bhtd,bhde->bhte', qc, c_mem) + jnp.einsum('bhts,bhse->bhte', s, vc)
        den = w_inter * jnp.einsum('bhtd,bhd->bht', qc, n_mem) + s.sum(-1)
        h = num / jnp.maximum(jnp.abs(den), jnp.exp(-m_t))[..., None]
        b_last = b[..., -1]
        d_last = b_last[..., None] - b + lic
        m_new = jnp.maximum(b_last + m_prev, d_last.max(-1))
        w_s = jnp.exp(d_last - m_new[..., None])[..., None] * kc
        decay = jnp.exp(b_last + m_prev - m_new)
        c_new = decay[..., None, None] * c_mem + jnp.einsum('bhsd,bhse->bhde', w_s, vc)
        n_new = decay[..., None] * n_mem + w_s.sum(2)
        return (c_new, n_new, m_new), h

    state, hs = lax.scan(step, state, (chunks(q), chunks(k), chunks(v), chunks(log_i), chunks(log_f)))
    return jnp.moveaxis(hs, 0, 2).reshape(bsz, nh, n, dh), state

def mlstm_inputs(u, conv_w, b_gate):
    bsz, n, _ = u.shape
    qk = short_conv(u[..., :2 * M_WIDTH], conv_w)
    q = to_heads(qk[..., :M_WIDTH])
    k = to_heads(qk[..., M_WIDTH:]) * (M_HEAD_DIM ** -0.5)
    v = to_heads(u[..., 2 * M_WIDTH:3 * M_WIDTH])
    g = (u[..., GATE_OFF:] + b_gate).astype(f32).reshape(bsz, n, 4, M_HEADS)
    g = jnp.transpose(g, (2, 0, 3, 1))
    return q, k, v, (g[0], jax.nn.log_sigmoid(g[1]), g[2], jax.nn.log_sigmoid(g[3]))

def multiscale_pool(u, pool_w, pool_scale):
    bsz, n, _ = u.shape
    ug = u.astype(f32).reshape(bsz, n, P_GROUPS, P_GROUP_DIM)
    csum = jnp.concatenate([jnp.zeros_like(ug[:, :1]), jnp.cumsum(ug, axis=1)], axis=1)
    t = jnp.arange(n)[:, None]
    half = jnp.array(P_WINDOWS, jnp.int32)[None, :] // 2
    lo = jnp.clip(t - half, 0, n)
    hi = jnp.clip(t + half, 0, n)
    gi = jnp.arange(P_GROUPS)[None, :]
    win_sum = csum[:, hi, gi] - csum[:, lo, gi]
    mean = win_sum / (hi - lo).astype(f32)[None, :, :, None]
    mixed = jnp.einsum('bngc,gcd->bngd', mean - ug, pool_w.astype(f32))
    return mixed.reshape(bsz, n, P_WIDTH) * pool_scale

def head_rmsnorm(h, w):
    bsz, n, _ = h.shape
    hh = h.reshape(bsz, n, M_HEADS, M_HEAD_DIM)
    hh = hh * lax.rsqrt(jnp.mean(hh * hh, -1, keepdims=True) + EPS)
    return hh.reshape(bsz, n, M_WIDTH) * w

def mlstm_pool_output(u, h, mnorm_w, pool_w, pool_scale, w_out):
    bsz, n, _ = u.shape
    o_gate = jax.nn.sigmoid(u[..., 3 * M_WIDTH:4 * M_WIDTH].astype(f32))
    h = jnp.transpose(h, (0, 2, 1, 3)).reshape(bsz, n, M_WIDTH) * o_gate
    y_m = head_rmsnorm(h, mnorm_w) * jax.nn.silu(u[..., 4 * M_WIDTH:5 * M_WIDTH].astype(f32))
    p0 = 5 * M_WIDTH
    y_p = multiscale_pool(u[..., p0:p0 + P_WIDTH], pool_w, pool_scale) * jax.nn.silu(
        u[..., p0 + P_WIDTH:p0 + 2 * P_WIDTH].astype(f32))
    return jnp.concatenate([y_m, y_p], -1).astype(u.dtype) @ w_out

def mlstm_pool_mixer(hx, hc, w_in, b_gate, conv_w, mnorm_w, pool_w, pool_scale, w_out, need_ctx):
    ux, uc = hx @ w_in, hc @ w_in
    qx, kx, vx, (lif_x, lff_x, lib_x, lfb_x) = mlstm_inputs(ux, conv_w, b_gate)
    qc, kc, vc, (lif_c, lff_c, lib_c, lfb_c) = mlstm_inputs(uc, conv_w, b_gate)
    bsz = hx.shape[0]
    zero = (jnp.zeros((bsz, M_HEADS, M_HEAD_DIM, M_HEAD_DIM), f32),
            jnp.zeros((bsz, M_HEADS, M_HEAD_DIM), f32),
            jnp.zeros((bsz, M_HEADS), f32))
    rev = lambda a: jnp.flip(a, axis=2)
    hc_f, st_f = mlstm_chunkwise(qc, kc, vc, lif_c, lff_c, zero)
    hx_f, _ = mlstm_chunkwise(qx, kx, vx, lif_x, lff_x, st_f)
    hc_b, st_b = mlstm_chunkwise(rev(qc), rev(kc), rev(vc), rev(lib_c), rev(lfb_c), zero)
    hx_b, _ = mlstm_chunkwise(rev(qx), rev(kx), rev(vx), rev(lib_x), rev(lfb_x), st_b)
    yx = mlstm_pool_output(ux, hx_f + rev(hx_b), mnorm_w, pool_w, pool_scale, w_out)
    yc = mlstm_pool_output(uc, hc_f + rev(hc_b), mnorm_w, pool_w, pool_scale, w_out) if need_ctx else None
    return yx, yc

def axial_rope(n):
    rows = n // GRID_W
    row = jnp.repeat(jnp.arange(rows), GRID_W).astype(f32)
    col = jnp.tile(jnp.arange(GRID_W), rows).astype(f32)
    n_freq = A_HEAD_DIM // 4
    inv = ROPE_BASE ** (-jnp.arange(n_freq, dtype=f32) / n_freq)
    ang = jnp.concatenate([row[:, None] * inv, col[:, None] * inv], -1)
    return jnp.cos(ang), jnp.sin(ang)

def apply_rope(x, cos, sin):
    xf = x.astype(f32)
    x1, x2 = xf[..., 0::2], xf[..., 1::2]
    c, s = cos[None, :, None, :], sin[None, :, None, :]
    return jnp.stack([x1 * c - x2 * s, x1 * s + x2 * c], -1).reshape(x.shape).astype(x.dtype)

def gqa_scores(q, k):
    return jnp.einsum('bqkgd,bskd->bkgqs', q, k).astype(f32) * (A_HEAD_DIM ** -0.5)

def window_attention(q, k, v, k_ctx, v_ctx, sink):
    bsz, n = q.shape[:2]
    n_ctx = k_ctx.shape[1]
    pad = ((0, 0), (A_WINDOW, A_WINDOW), (0, 0), (0, 0))
    kp, vp = jnp.pad(k, pad), jnp.pad(v, pad)
    qg = q.reshape(bsz, n, A_KV_HEADS, A_GROUP, A_HEAD_DIM)
    sink_l = sink.reshape(1, A_KV_HEADS, A_GROUP, 1, 1).astype(f32)

    def block(bi):
        start = bi * A_BLOCK
        qb = lax.dynamic_slice_in_dim(qg, start, A_BLOCK, axis=1)
        kb = lax.dynamic_slice_in_dim(kp, start, A_BAND, axis=1)
        vb = lax.dynamic_slice_in_dim(vp, start, A_BAND, axis=1)
        qi = start + jnp.arange(A_BLOCK)
        kj = start - A_WINDOW + jnp.arange(A_BAND)
        ok = (jnp.abs(qi[:, None] - kj[None, :]) <= A_WINDOW) & (kj >= 0) & (kj < n)
        s_lat = jnp.where(ok, gqa_scores(qb, kb), -jnp.inf)
        s_ctx = gqa_scores(qb, k_ctx)
        sk = jnp.broadcast_to(sink_l, s_ctx.shape[:-1] + (1,))
        p = jax.nn.softmax(jnp.concatenate([s_lat, s_ctx, sk], -1), axis=-1)
        o = (jnp.einsum('bkgqs,bskd->bqkgd', p[..., :A_BAND].astype(v.dtype), vb)
             + jnp.einsum('bkgqs,bskd->bqkgd', p[..., A_BAND:A_BAND + n_ctx].astype(v.dtype), v_ctx))
        return o.reshape(bsz, A_BLOCK, A_WIDTH)

    out = lax.map(block, jnp.arange(n // A_BLOCK))
    return jnp.moveaxis(out, 0, 1).reshape(bsz, n, A_WIDTH)

def context_attention(q, k, v, sink):
    bsz, n = q.shape[:2]
    s = gqa_scores(q.reshape(bsz, n, A_KV_HEADS, A_GROUP, A_HEAD_DIM), k)
    sk = jnp.broadcast_to(sink.reshape(1, A_KV_HEADS, A_GROUP, 1, 1).astype(f32), s.shape[:-1] + (1,))
    p = jax.nn.softmax(jnp.concatenate([s, sk], -1), axis=-1)
    o = jnp.einsum('bkgqs,bskd->bqkgd', p[..., :n].astype(v.dtype), v)
    return o.reshape(bsz, n, A_WIDTH)

def split_attn(u):
    bsz, n, _ = u.shape
    q = u[..., :A_WIDTH].reshape(bsz, n, A_HEADS, A_HEAD_DIM)
    k = u[..., A_WIDTH:A_WIDTH + A_KV_WIDTH].reshape(bsz, n, A_KV_HEADS, A_HEAD_DIM)
    v = u[..., A_WIDTH + A_KV_WIDTH:A_WIDTH + 2 * A_KV_WIDTH].reshape(bsz, n, A_KV_HEADS, A_HEAD_DIM)
    z = u[..., A_WIDTH + 2 * A_KV_WIDTH:]
    return q, k, v, z

def window_attention_mixer(hx, hc, w_in, sink, w_out, need_ctx):
    qx, kx, vx, zx = split_attn(hx @ w_in)
    qc, kc, vc, zc = split_attn(hc @ w_in)
    cos, sin = axial_rope(hx.shape[1])
    qx, kx = apply_rope(qx, cos, sin), apply_rope(kx, cos, sin)
    ox = window_attention(qx, kx, vx, kc, vc, sink)
    yx = (ox * jax.nn.silu(zx)) @ w_out
    yc = (context_attention(qc, kc, vc, sink) * jax.nn.silu(zc)) @ w_out if need_ctx else None
    return yx, yc

def second_inputs(seed: int = 0) -> dict:
    key = jax.random.key(seed)
    ks = jax.random.split(key, 20)
    nrm = lambda k, shape, s: jax.random.normal(k, shape, f32) * s
    kg = jax.random.split(ks[9], 2)
    i_bias = nrm(kg[0], (N_EVEN, 2, M_HEADS), 0.1)
    f_bias = jnp.linspace(3.0, 6.0, M_HEADS, dtype=f32) + nrm(kg[1], (N_EVEN, 2, M_HEADS), 0.1)
    return {
        'x': nrm(ks[0], (BATCH, SEQ, D_MODEL), 1.0),
        'c': nrm(ks[1], (BATCH, D_MODEL), 1.0),
        'ctx': nrm(ks[2], (BATCH, CTX_LEN, D_MODEL), 1.0),
        'c_ctx': nrm(ks[3], (D_MODEL,), 1.0),
        'w_mod': nrm(ks[4], (DEPTH_2, D_MODEL, 3 * D_MODEL), 0.5 * D_MODEL ** -0.5),
        'b_mod': nrm(ks[5], (DEPTH_2, 3 * D_MODEL), 0.01),
        'g_pre': 1.0 + nrm(ks[6], (DEPTH_2, D_MODEL), 0.02),
        'g_post': 1.0 + nrm(ks[7], (DEPTH_2, D_MODEL), 0.02),
        'ab_w_in': nrm(ks[8], (N_EVEN, D_MODEL, AB_IN), D_MODEL ** -0.5),
        'ab_b_gate': jnp.stack([i_bias, f_bias], axis=2).reshape(N_EVEN, N_GATE),
        'ab_conv': nrm(ks[10], (N_EVEN, M_CONV, 2 * M_WIDTH), M_CONV ** -0.5),
        'ab_mnorm': 1.0 + nrm(ks[11], (N_EVEN, M_WIDTH), 0.02),
        'ab_pool_w': nrm(ks[12], (N_EVEN, P_GROUPS, P_GROUP_DIM, P_GROUP_DIM), P_GROUP_DIM ** -0.5),
        'ab_pool_scale': 1.0 + nrm(ks[13], (N_EVEN, P_WIDTH), 0.02),
        'ab_w_out': nrm(ks[14], (N_EVEN, AB_WIDTH, D_MODEL), AB_WIDTH ** -0.5),
        'c_w_in': nrm(ks[15], (N_ODD, D_MODEL, C_IN), D_MODEL ** -0.5),
        'c_sink': nrm(ks[16], (N_ODD, A_HEADS), 1.0),
        'c_w_out': nrm(ks[17], (N_ODD, A_WIDTH, D_MODEL), A_WIDTH ** -0.5),
    }

def second_block(x, c, ctx, c_ctx, w_mod, b_mod, g_pre, g_post, ab_w_in, ab_b_gate, ab_conv, ab_mnorm,
              ab_pool_w, ab_pool_scale, ab_w_out, c_w_in, c_sink, c_w_out):
    for l in range(DEPTH_2):
        j = l // 2
        last = l == DEPTH_2 - 1
        shift, scale, gate = jnp.split(jax.nn.silu(c) @ w_mod[l] + b_mod[l], 3, axis=-1)
        shift_c, scale_c, gate_c = jnp.split(jax.nn.silu(c_ctx) @ w_mod[l] + b_mod[l], 3, axis=-1)
        hx = rmsnorm(x, g_pre[l]) * (1 + scale[:, None]) + shift[:, None]
        hc = rmsnorm(ctx, g_pre[l]) * (1 + scale_c) + shift_c
        if l % 2 == 0:
            yx, yc = mlstm_pool_mixer(hx, hc, ab_w_in[j], ab_b_gate[j], ab_conv[j], ab_mnorm[j],
                                      ab_pool_w[j], ab_pool_scale[j], ab_w_out[j], not last)
        else:
            yx, yc = window_attention_mixer(hx, hc, c_w_in[j], c_sink[j], c_w_out[j], not last)
        x = x + gate[:, None] * rmsnorm(yx, g_post[l])
        if not last:
            ctx = ctx + gate_c * rmsnorm(yc, g_post[l])
    return x


def setup_inputs(seed=0):
    out = dict(first_inputs(seed))
    for name, value in second_inputs(seed + 1).items():
        if name != "x":
            out[name + "_2"] = value
    return out


def reference(
    x, c, ctx, c_ctx, ada_w, ada_b, norm1_g, norm2_g, w_in, hgrn_lb, hgrn_norm_g, hy_conv_w,
    hy_conv_b, hy_filt_w1, hy_filt_b1, hy_filt_freq1, hy_filt_w2, hy_filt_b2, hy_filt_freq2,
    hy_filt_w3, hy_d, w_proj_a, w_proj_b, w_out, moe_router_g_w, moe_router_g_b, moe_router_e_w,
    moe_router_e_b, moe_w_gate, moe_w_up, moe_w_down, final_norm_g, c_2, ctx_2, c_ctx_2,
    w_mod_2, b_mod_2, g_pre_2, g_post_2, ab_w_in_2, ab_b_gate_2, ab_conv_2, ab_mnorm_2,
    ab_pool_w_2, ab_pool_scale_2, ab_w_out_2, c_w_in_2, c_sink_2, c_w_out_2,
):
    x = first_block(
        x, c, ctx, c_ctx, ada_w, ada_b, norm1_g, norm2_g, w_in, hgrn_lb, hgrn_norm_g, hy_conv_w,
        hy_conv_b, hy_filt_w1, hy_filt_b1, hy_filt_freq1, hy_filt_w2, hy_filt_b2, hy_filt_freq2,
        hy_filt_w3, hy_d, w_proj_a, w_proj_b, w_out, moe_router_g_w, moe_router_g_b,
        moe_router_e_w, moe_router_e_b, moe_w_gate, moe_w_up, moe_w_down, final_norm_g,
    )
    return second_block(
        x, c_2, ctx_2, c_ctx_2, w_mod_2, b_mod_2, g_pre_2, g_post_2, ab_w_in_2, ab_b_gate_2,
        ab_conv_2, ab_mnorm_2, ab_pool_w_2, ab_pool_scale_2, ab_w_out_2, c_w_in_2, c_sink_2,
        c_w_out_2,
    )


_drawn_inputs = setup_inputs


def setup_inputs(seed=0):
    import zlib

    import numpy as np

    out = dict(_drawn_inputs(seed))
    spreads = {}
    factors = {'ctx': 7.865,
     'c_ctx': 8.0,
     'ada_b': 2.954,
     'norm1_g': 3.154,
     'hgrn_lb': 4.976,
     'hgrn_norm_g': 6.464,
     'hy_conv_b': 8.0,
     'hy_filt_b1': 3.851,
     'hy_filt_freq1': 5.291,
     'hy_filt_freq2': 6.272,
     'moe_router_g_b': 8.0,
     'moe_router_e_b': 4.723,
     'b_mod_2': 2.702,
     'g_pre_2': 3.625,
     'g_post_2': 6.809,
     'ab_mnorm_2': 8.0,
     'ab_pool_scale_2': 8.0,
     'c_sink_2': 64.0}
    for name, (base, spread) in spreads.items():
        noise = np.random.default_rng([zlib.crc32(name.encode()), seed]).standard_normal(out[name].shape)
        drawn = base * np.exp(spread * noise) if base else spread * noise
        out[name] = __import__('jax').numpy.asarray(drawn.astype(out[name].dtype))
    for name, factor in factors.items():
        out[name] = (out[name] * factor).astype(out[name].dtype)
    return out
```

```python
from contextlib import ExitStack

import numpy as np
import concourse.bass as bass
from concourse import mybir

F32 = mybir.dt.float32
I32 = mybir.dt.int32
ALU = mybir.AluOpType
ACT = mybir.ActivationFunctionType
AXX = mybir.AxisListType.X

P = 128
D = 1024
DT = D // P
T = 256
TT = T // P
T2 = 2 * T
EPS = 1e-6
BIG = 1e30

H1, DK, CHUNK = 4, 128, 32
NCH = T // CHUNK
HYW = 512
NG, NE, FE = 4, 8, 512
NX = NG * NE
CAP = 64
MH, MD = 4, 256
POOLS = (2, 4, 8, 16)
PADP = 8
AH, AKV, AD = 16, 4, 64

SLOT = DT * 512
RING = 3

_COLS = [("ada_b", 48), ("n1g", 8), ("n2g", 8), ("fng", 8), ("lb", 16), ("hng", 1), ("cw", 36), ("cb", 12),
         ("hyd", 4), ("bm2", 48), ("gpre", 16), ("gpost", 16), ("acv", 48), ("mng", 8), ("psc", 8), ("gb", 1)]
COL = {}
_at = 0
for _n, _w in _COLS:
    COL[_n] = (_at, _w)
    _at += _w
NVEC = _at


def shape_constants():
    c = {}
    t = np.arange(T)
    quarter = D // 4
    omega = (1.0 / (10000.0 ** (np.arange(quarter, dtype=np.float32) / np.float32(quarter)))).astype(np.float32)

    def axis_emb(pos):
        a = pos.astype(np.float32)[:, None] * omega[None, :]
        return np.concatenate([np.sin(a), np.cos(a)], -1)

    pos = np.concatenate([axis_emb(t // 64), axis_emb(t % 64)], -1).astype(np.float32)
    c["pos"] = pos.T.reshape(DT, P, T).transpose(1, 0, 2)
    n = 2 * T
    f = np.arange(T)
    ang = 2 * np.pi * ((np.arange(n)[:, None] * f[None, :]) % n) / n
    re, im = np.cos(ang), -np.sin(ang)
    nyq = np.where(np.arange(n) % 2 == 0, 1.0, -1.0)
    im_n = im.copy()
    im_n[:, 0] = nyq
    fu = np.concatenate([re, im_n], 1)[:T]
    c["dft_u"] = fu.reshape(TT, P, 2 * T).transpose(1, 0, 2)
    im_0 = im.copy()
    im_0[:, 0] = 0.0
    re_n = re[:, :P].copy()
    re_n[:, 0] = nyq
    fk = np.concatenate([re, im_0, re_n], 1)
    fwd = fk[:T]
    bwd = fk[(n - np.arange(T)) % n].copy()
    bwd[0] = 0.0
    c["dft_k"] = np.stack([fwd, bwd]).reshape(2, TT, P, 5 * P).transpose(2, 0, 1, 3)
    wt = np.full(T, 2.0)
    wt[0] = 1.0
    gr = (wt[:, None] * np.cos(ang[:T].T)) / n
    gi = (-2.0 * np.sin(ang[:T].T)) / n
    gi[0] = nyq[:T] / n
    c["idft"] = np.concatenate([gr, gi]).reshape(4, P, T).transpose(1, 0, 2)
    tl = np.linspace(0.0, 1.0, T, dtype=np.float32)[:, None]
    bands = 16
    a2 = (2.0 * np.pi * np.arange(T, dtype=np.float32) / T)[:, None] * \
        np.linspace(1e-4, bands - 1, bands, dtype=np.float32)[None, :]
    c["zfeat"] = np.concatenate([tl, np.cos(a2), -np.sin(a2)], -1).T
    deltas = np.abs(np.linspace(np.log(1e-2) / 1.5, np.log(1e-2) / 0.3, HYW))
    c["decay"] = np.exp(-tl * deltas[None, :]).reshape(TT, P, HYW).transpose(1, 0, 2)
    s, q = np.arange(P)[:, None], np.arange(P)[None, :]
    same = s // CHUNK == q // CHUNK
    c["gla_mask"] = np.stack([same & (s <= q), same & (s >= q)], 1).astype(np.int32)
    c["ident"] = np.eye(P)
    c["tri"] = np.triu(np.ones((P, P)))
    c["slot_no"] = np.tile(np.arange(CAP), (P, 1))
    c["tie"] = np.tile(np.arange(8, 0, -1), (P, 1))
    c["m_mask"] = np.stack([np.where(s <= q, 0.0, -BIG), np.where(s >= q, 0.0, -BIG)], 1)
    sel = np.zeros((MH, MH, P))
    sel[np.arange(MH), np.arange(MH)] = 1.0
    c["m_sel"] = sel
    inv = []
    for w in POOLS:
        inv.append(1.0 / (np.clip(t + w // 2, 0, T) - np.clip(t - w // 2, 0, T)))
    c["pool_inv"] = np.tile(np.stack(inv)[None], (P, 1, 1))
    n_freq = AD // 4
    invf = (10000.0 ** (-np.arange(n_freq, dtype=np.float32) / n_freq)).astype(np.float32)
    ang = np.concatenate([(t // 64)[:, None].astype(np.float32) * invf, (t % 64)[:, None].astype(np.float32) * invf], -1)
    cos = np.repeat(np.cos(ang), 2, axis=1).T
    sin = np.repeat(np.sin(ang), 2, axis=1).T
    sin[0::2] *= -1.0
    c["rope"] = np.stack([np.tile(cos, (2, 1)), np.tile(sin, (2, 1))], 1)
    c["swap"] = np.eye(P)[np.arange(P) ^ 1]
    i, j = np.arange(T)[:, None], np.arange(T)[None, :]
    c["a_mask"] = np.where(np.abs(i - j) <= 128, 0.0, -BIG).reshape(TT, P, T).transpose(1, 0, 2)
    return {k: np.ascontiguousarray(v if v.dtype == np.int32 else v.astype(np.float32)) for k, v in c.items()}


def layout(inputs):
    i = {k: np.asarray(v) for k, v in inputs.items()}

    def cols(v):
        return v.reshape(-1, P).T

    def tokens(v):
        return v.reshape(T, DT, P).transpose(2, 1, 0)

    gb, gate_w = np.zeros(P, np.float32), np.zeros((P, DT, P), np.float32)
    off = i["ab_w_in_2"].shape[2] - 4 * MH
    for n, at in enumerate((0, 64, 32, 96)):
        s = slice(n * MH, (n + 1) * MH)
        gb[at:at + MH] = i["ab_b_gate_2"][0, s]
        gate_w[:, :, at:at + MH] = i["ab_w_in_2"][0, :, off:][:, s].reshape(DT, P, MH).transpose(1, 0, 2)
    vectors = {"ada_b": i["ada_b"], "n1g": i["norm1_g"], "n2g": i["norm2_g"], "fng": i["final_norm_g"], "lb": i["hgrn_lb"],
               "hng": i["hgrn_norm_g"], "cw": i["hy_conv_w"], "cb": i["hy_conv_b"], "hyd": i["hy_d"], "bm2": i["b_mod_2"],
               "gpre": i["g_pre_2"], "gpost": i["g_post_2"], "acv": i["ab_conv_2"], "mng": i["ab_mnorm_2"],
               "psc": i["ab_pool_scale_2"], "gb": gb}
    a = shape_constants()
    a["vecs"] = np.concatenate([cols(vectors[n]) for n, _ in _COLS], 1)
    a["gate_w"] = gate_w
    a["cvec"] = np.stack([v.reshape(DT, P) for v in (i["c"], i["c_ctx"], i["c_2"], i["c_ctx_2"])]).transpose(2, 1, 0)
    a["x"], a["ctx"], a["ctx_2"] = tokens(i["x"]), tokens(i["ctx"]), tokens(i["ctx_2"])
    a["fcol"] = np.stack([i["hy_filt_b1"][0], i["hy_filt_freq1"][0], i["hy_filt_b2"][0], i["hy_filt_freq2"][0]], 1)
    a["router_w"] = np.concatenate([i["moe_router_g_w"][0].reshape(DT, P, NG)]
                                   + [i["moe_router_e_w"][0, g].reshape(DT, P, NE) for g in range(NG)], 2).transpose(1, 0, 2)
    a["router_b"] = np.concatenate([i["moe_router_g_b"].reshape(-1), i["moe_router_e_b"].reshape(-1)])
    a["c_sink_2"] = i["c_sink_2"].reshape(-1)
    for n in ("ada_w", "w_in", "w_proj_a", "w_proj_b", "w_out", "hy_filt_w1", "hy_filt_w2", "hy_filt_w3", "ab_w_in_2",
              "ab_w_out_2", "c_w_in_2", "c_w_out_2"):
        a[n] = i[n][0]
    heads = [8 * m + g + 4 * half for m in range(2) for g in range(4) for half in range(2)]
    order = np.concatenate([np.arange(h * AD, (h + 1) * AD) for h in heads])
    w = a["c_w_in_2"]
    a["c_w_in_2"] = np.concatenate([w[:, order], w[:, D:D + 512], w[:, D + 512:][:, order]], 1)
    a["c_w_out_2"] = a["c_w_out_2"][order]
    a["w_mod_2"] = np.concatenate([i["w_mod_2"][0], i["w_mod_2"][1]], 1)
    a["ab_pool_w_2"] = i["ab_pool_w_2"][0]
    for n in ("moe_w_gate", "moe_w_up", "moe_w_down"):
        a[n] = i[n][0].reshape((NG * NE,) + i[n].shape[3:])
    return {k: np.ascontiguousarray(v) for k, v in a.items()}


class Arena:

    def __init__(self, tensor, words):
        self.tensor, self.words, self.at = tensor, words, 0

    def mark(self):
        return self.at

    def to(self, mark):
        self.at = mark

    def take(self, *shape):
        n = int(np.prod(shape))
        n_even = n + n % 2
        assert self.at + n_even <= self.words, (self.at, n_even, self.words)
        flat = self.tensor[:, self.at:self.at + n]
        self.at += n_even
        if len(shape) == 1:
            return flat
        names = "abcdef"[:len(shape)]
        spec = f"p ({' '.join(names)}) -> p {' '.join(names)}"
        return flat.rearrange(spec, **{k: v for k, v in zip(names[1:], shape[1:])})


def bc(ap, shape):
    return ap.broadcast_to(shape)


def build(nc, d, out):
    ctx = ExitStack()
    with ctx:
        def sb(name, shape, dt=F32):
            return ctx.enter_context(nc.sbuf_tensor(name, shape, dt))

        def sem(name):
            return ctx.enter_context(nc.semaphore(name))

        ident = sb("ident", [P, P])
        ones = sb("ones", [P, P])
        epsc = sb("epsc", [P, 1])
        vecs = sb("vecs", [P, NVEC])
        cvec = sb("cvec", [P, DT, 4])
        csil = sb("csil", [P, 2, DT, 32])
        mod1 = sb("mod1", [P, 48, 2])
        mod2 = sb("mod2", [P, 48, 2])
        coef = sb("coef", [P, 2, DT])
        gcoef = sb("gcoef", [P, 2, DT])
        X = sb("X", [P, DT, T2])
        H = sb("H", [P, DT, T2])
        rstd = sb("rstd", [P, T2])
        ring = sb("ring", [P, RING, SLOT])
        router_w = sb("router_w", [P, DT, 36])
        router_b = sb("router_b", [P, 36])
        tie = sb("tie", [P, 8])
        gate_w = sb("gate_w", [P, DT, P])
        sink_b = sb("sink_b", [P, AH])
        mcols = sb("mcols", [P, 4, 4, 2, MH])
        decay_b = sb("decay_b", [P, 2, MH, 4])
        WORK = 33100
        work = sb("work", [P, WORK])
        ar = Arena(work, WORK)
        bank = [ctx.enter_context(nc.psum_tensor(f"bank{i}", [P, 512], F32)) for i in range(8)]

        def vec(name, a=0, b=None):
            at, w = COL[name]
            return vecs[:, at + a:at + (w if b is None else b)]

        slot_filled = [sem(f"slot_filled{i}") for i in range(RING)]
        last_use = {}
        stage_done = sem("stage_done")
        dve_step, act_step = sem("dve_step"), sem("act_step")
        sq_ready, sumsq_done, std_done = sem("sq_ready"), sem("sumsq_done"), sem("std_done")
        scaled, hmod = sem("scaled"), sem("hmod")
        small_in = sem("small_in")
        out_done = sem("out_done")

        class Chain:

            def __init__(self, eng, s):
                self.eng, self.s, self.n = eng, s, 0

            def link(self, ins):
                self.n += 1
                ins.then_inc(self.s, 1)
                self.eng.wait_ge(self.s, self.n)

        stages = {"pe": 0, "act": 0, "dve": 0}

        def stage_end(eng, who):
            stages[who] += 1
            eng.drain().then_inc(stage_done, 1)
            eng.wait_ge(stage_done, 3 * stages[who])

        def tall(w, c, width=512):
            return w.rearrange("(k p) n -> p k n", p=P)[:, :, c * width:(c + 1) * width]

        def wide(w, r):
            return w[r * 512:(r + 1) * 512, :].rearrange("(k p) n -> p k n", p=P)

        chunks = []
        slot_until = [(-RING + s, None) for s in range(RING)]
        slot_turns = [0] * RING
        now = [0]

        def plan(src, steps=1, held=1):
            s = min(range(RING), key=lambda s: slot_until[s][0])
            slot_turns[s] += 1
            chunks.append((src, s, slot_turns[s], slot_until[s][1]))
            slot_until[s] = (now[0] + held - 1, len(chunks) - 1)
            now[0] += steps
            return len(chunks) - 1

        N_MOD, N_MOD_1 = 24, 4
        HOSTED = (3, 3, 4, 3, 2)
        N_MOD_2 = N_MOD_1 + sum(HOSTED)

        def mod_src(m):
            return tall(d["ada_w"], m) if m < 12 else tall(d["w_mod_2"], m - 12)

        mod_chunk = [plan(mod_src(m)) for m in range(N_MOD_1)]
        in_chunk = []
        for c in range(12):
            if c == len(HOSTED):
                for m in range(N_MOD_2, 24):
                    mod_chunk.append(plan(mod_src(m)))
            hosted = HOSTED[c] if c < len(HOSTED) else 0
            in_chunk.append(plan(tall(d["w_in"], c), steps=1, held=7))
            for i in range(hosted):
                mod_chunk.append(plan(mod_src(len(mod_chunk)), steps=2))
            now[0] += 2 * max(0, 4 - hosted)
        assert len(mod_chunk) == N_MOD
        pa_chunk, pb_chunk = plan(wide(d["w_proj_a"], 0)), plan(wide(d["w_proj_b"], 0))
        out_chunk = [plan(tall(d["w_out"], c)) for c in range(2)]
        N_FIRST = len(chunks)
        moe_slots = sorted(range(RING), key=lambda s: slot_until[s][0])
        before_moe = [slot_until[s][1] for s in moe_slots]
        n_moe = 3 * NG * NE
        AB = (0, 1, 2, 3, 4, 5, 10, 11, 12, 13, 6, 7, 8, 9)
        second = [tall(d["ab_w_in_2"], c) for c in AB] + [d["ab_w_out_2"].rearrange("(k p) n -> p k n", p=P)[:, :, r * 256:(r + 1) * 256] for r in range(4)]
        second += [tall(d["c_w_in_2"], c) for c in range(5)] + [tall(d["c_w_out_2"], c) for c in range(2)]
        AT_SECOND = N_FIRST
        for s, i in zip(moe_slots, range(RING)):
            slot_until[s] = (now[0] + i, "experts")
        now[0] += RING
        for src in second:
            plan(src)
        AT_C = AT_SECOND + 18
        AT_CO = AT_C + 5

        def chunk_wait(pe, c):
            _, s, turns, _ = chunks[c]
            pe.wait_ge(slot_filled[s], 16 * turns)

        def slot_k(c, k, a, b):
            return ring[:, chunks[c][1], k * 512 + a:k * 512 + b]

        def slot_w(c, k, a, b):
            return ring[:, chunks[c][1], k * 1024 + a:k * 1024 + b]

        def load_chunk(sp, c):
            src, s, _, displaced = chunks[c]
            if displaced is not None:
                sp.wait_ge(*last_use[displaced])
            dst = ring[:, s, :].rearrange("p (k n) -> p k n", n=src.shape[2])
            sp.dma_start(dst, src).then_inc(slot_filled[s], 16)

        norm_use = {"pe": 0, "act": 0, "dve": 0}

        def norm_pe(pe, src, n):
            u = norm_use["pe"]
            norm_use["pe"] += 1
            for k in range(DT):
                pe.wait_ge(sq_ready, DT * u + k + 1)
                mm = nc.tensor.matmul(bank[7][:, 0:n], ones[:], src[:, k, 0:n], start=(k == 0), stop=(k == DT - 1))
            mm.then_inc(sumsq_done, 1)

        def squares_act(act, src, sq, n):
            for k in range(DT):
                nc.scalar.activation(sq[:, k, 0:n], src[:, k, 0:n], ACT.Square).then_inc(sq_ready, 1)

        def norm_act(act, src, sq, n):
            squares_act(act, src, sq, n)
            std_act(act, n)

        def std_act(act, n):
            u = norm_use["act"]
            norm_use["act"] += 1
            act.wait_ge(sumsq_done, u + 1)
            nc.scalar.activation(rstd[:, 0:n], bank[7][:, 0:n], ACT.Sqrt, bias=epsc[:], scale=1.0 / D).then_inc(std_done, 1)

        def norm_dve(dve, chain, n):
            u = norm_use["dve"]
            norm_use["dve"] += 1
            dve.wait_ge(std_done, u + 1)
            chain.link(nc.vector.reciprocal(rstd[:, 0:n], rstd[:, 0:n]))

        mod_use = {"act": 0, "dve": 0}

        def coef_dve(chain, g, mod, at_scale, both):
            for j in range(1 + both):
                chain.link(nc.vector.tensor_scalar(coef[:, j, :], mod[:, at_scale:at_scale + DT, j], 1.0, None, ALU.add))
                chain.link(nc.vector.tensor_tensor(coef[:, j, :], coef[:, j, :], g, ALU.mult))

        def modulate_dve(dve, both):
            for k in range(DT):
                for j in range(1 + both):
                    s = slice(j * T, (j + 1) * T)
                    nc.vector.scalar_tensor_tensor(out=H[:, k, s], in0=X[:, k, s], scalar=coef[:, j, k:k + 1],
                                                   in1=rstd[:, s], op0=ALU.mult, op1=ALU.mult).then_inc(scaled, 1)

        def modulate_act(act, mod, at_shift, both):
            for k in range(DT):
                for j in range(1 + both):
                    s = slice(j * T, (j + 1) * T)
                    mod_use["act"] += 1
                    act.wait_ge(scaled, mod_use["act"])
                    nc.scalar.activation(H[:, k, s], H[:, k, s], ACT.Identity,
                                         bias=mod[:, at_shift + k, j:j + 1]).then_inc(hmod, 1)


        m0 = ar.mark()
        hyk = ar.take(5, 512)
        dft_u = ar.take(TT, 2 * T)
        idft = ar.take(4, T)
        modrow = ar.take(2, P)
        lbc, omlb, lbt = ar.take(8), ar.take(8), ar.take(2, 8)
        m_first = ar.mark()
        pos = ar.take(DT, T)
        dft_k = ar.take(2, TT, 5 * P)
        decay = ar.take(TT, HYW)
        zfeat = ar.take(T)
        fw1, fw2, fw3, fcol = ar.take(64), ar.take(64), ar.take(2 * HYW), ar.take(4)
        farg, fturn = ar.take(T), ar.take(T)
        fh = ar.take(2, T)
        hfilt = ar.take(TT, 2, HYW)
        cvec_in, vecs_in = sem("cvec_in"), sem("vecs_in")
        x_in, csil_ready, x_ready, filt_in = sem("x_in"), sem("csil_ready"), sem("x_ready"), sem("filt_in")
        taps_in = sem("taps_in")
        mrow_mm, mrow_out, mcol_mm, mcol_out = sem("mrow_mm"), sem("mrow_out"), sem("mcol_mm"), sem("mcol_out")
        f_mm, f_lin, f_sin, f_taps, k_mm = sem("f_mm"), sem("f_lin"), sem("f_sin"), sem("f_taps"), sem("k_mm")
        lb_ready, lb_e = sem("lb_ready"), sem("lb_e")
        K_BANKS = (0, 1, 2, 3, 6)

        def loads_sync(sp):
            sp.dma_start(X[:, :, 0:T], d["x"]).then_inc(x_in, 16)
            sp.dma_start(pos, d["pos"]).then_inc(x_in, 16)
            sp.dma_start(X[:, :, T:T2], d["ctx"]).then_inc(x_in, 16)

        def loads_act(act):
            act.dma_start(cvec[:], d["cvec"]).then_inc(cvec_in, 16)
            for dst, src in ((zfeat[0:33, :], d["zfeat"]), (fw1[0:33, :], d["hy_filt_w1"]), (fcol[0:64, :], d["fcol"]),
                             (fw2[0:64, :], d["hy_filt_w2"]), (fw3[0:64, :], d["hy_filt_w3"])):
                act.dma_start(dst, src).then_inc(filt_in, 16)
            act.dma_start(vecs[:], d["vecs"]).then_inc(vecs_in, 16)
            act.dma_start(ident[:], d["ident"]).then_inc(vecs_in, 16)
            act.dma_start(decay, d["decay"]).then_inc(taps_in, 16)
            act.dma_start(dft_k, d["dft_k"]).then_inc(taps_in, 16)

        def loads_rest_sync(sp, c):
            if c == 0:
                sp.wait_ge(filt_in, 16 * 5)
            elif c == 1:
                sp.wait_ge(x_in, 16 * 3)

        SMALL = ((dft_u, d["dft_u"]), (idft, d["idft"]), (router_w[:], d["router_w"]), (tie[:], d["tie"]), (gate_w[:], d["gate_w"]),
                 (router_b[:], d["router_b"].partition_broadcast(P)), (sink_b[:], d["c_sink_2"].partition_broadcast(P)))
        N_SMALL = 16 * len(SMALL)

        def mod_rows_pe(pe, m):
            chunk_wait(pe, mod_chunk[m])
            if m >= 1:
                pe.wait_ge(mrow_out, m)
            for k in range(DT):
                for g in range(4):
                    mm = nc.tensor.matmul(bank[5][32 * g:32 * g + 32, 0:P], csil[:, m // 12, k, :], slot_k(mod_chunk[m], k, g * P, (g + 1) * P),
                                          start=(k == 0), stop=(k == DT - 1), skip_group_check=True)
            mm.then_inc(mrow_mm, 1)
            last_use[mod_chunk[m]] = (mrow_mm, m + 1)

        def mod_cols_pe(pe, m):
            pe.wait_ge(mrow_out, m + 1)
            if m == 0:
                pe.wait_ge(vecs_in, 32)
            else:
                pe.wait_ge(mcol_out, m)
            nc.tensor.transpose(bank[4][:, 0:P], modrow[:, m % 2, :], ident[:]).then_inc(mcol_mm, 1)

        def mod_step_dve(dve, m):
            dve.wait_ge(mrow_mm, m + 1)
            nc.vector.tensor_copy(modrow[:, m % 2, :], bank[5][:, 0:P]).then_inc(mrow_out, 1)
            dve.wait_ge(mcol_mm, m + 1)
            mod, b, at = (mod1, "ada_b", 4 * m) if m < 12 else (mod2, "bm2", 4 * (m - 12))
            nc.vector.tensor_tensor(mod[:, at:at + 4, :], bank[4][:, 0:P].rearrange("p (g r) -> p g r", r=32)[:, :, 0:2],
                                    bc(vec(b, at, at + 4).unsqueeze(2), [P, 4, 2]), ALU.add).then_inc(mcol_out, 1)

        def mod_pe(pe):
            def spectra(m0, m1):
                for m in range(m0, m1):
                    for j in range(2):
                        for t in range(TT):
                            mm = nc.tensor.matmul(bank[K_BANKS[m]][:], dft_k[:, j, t, m * P:(m + 1) * P], hfilt[:, t, j, :],
                                                  start=(j + t == 0), stop=(j + t == 2))
                    mm.then_inc(k_mm, 1)

            pe.wait_ge(filt_in, 16 * 5)
            nc.tensor.matmul(bank[6][0:64, 0:T], fw1[0:33, :], zfeat[0:33, :], start=True, stop=True).then_inc(f_mm, 1)
            pe.wait_ge(f_sin, 1)
            nc.tensor.matmul(bank[6][0:64, 0:T], fw2[0:64, :], fh[0:64, 0, :], start=True, stop=True).then_inc(f_mm, 1)
            norm_pe(pe, H, T2)
            pe.wait_ge(f_sin, 2)
            for t in range(TT):
                for j in range(2):
                    nc.tensor.matmul(bank[2 * t + j][:], fh[0:64, 1, t * P:(t + 1) * P], fw3[0:64, j * HYW:(j + 1) * HYW],
                                     start=True, stop=True).then_inc(f_mm, 1)
            pe.wait_ge(csil_ready, 3)
            mod_rows_pe(pe, 0)
            mod_cols_pe(pe, 0)
            pe.wait_ge(taps_in, 32)
            pe.wait_ge(f_taps, 4)
            for m in range(1, N_MOD_1):
                spectra(2 * (m - 1), min(5, 2 * m))
                mod_rows_pe(pe, m)
                mod_cols_pe(pe, m)

        def mod_act(act, chain):
            act.wait_ge(cvec_in, 16)
            act.wait_ge(csil_ready, 1)
            for blk in range(2):
                nc.scalar.activation(csil[:, blk, :, 0:2], cvec[:, :, 2 * blk:2 * blk + 2], ACT.Silu).then_inc(csil_ready, 1)
            act.wait_ge(f_lin, 1)
            nc.scalar.activation(fh[0:64, 0, :], farg[0:64, :], ACT.Sin).then_inc(f_sin, 1)
            act.wait_ge(x_ready, 1)
            squares_act(act, X, H, T2)
            act.wait_ge(f_lin, 2)
            nc.scalar.activation(fh[0:64, 1, :], farg[0:64, :], ACT.Sin).then_inc(f_sin, 1)
            std_act(act, T2)
            for dst, src in SMALL:
                act.dma_start(dst, src).then_inc(small_in, 16)
            act.wait_ge(lb_e, 1)
            nc.scalar.activation(lbt, lbt, ACT.Exp).then_inc(lb_ready, 1)
            for m in range(5):
                act.wait_ge(k_mm, m + 1)
                nc.scalar.copy(hyk[:, m, :], bank[K_BANKS[m]][:])
            modulate_act(act, mod1, 0, True)

        def mod_dve(dve, chain):
            nc.vector.memset(csil[:], 0.0).then_inc(csil_ready, 1)
            nc.vector.memset(ones[:], 1.0)
            chain.link(nc.vector.memset(epsc[:], EPS))
            C1 = 6.28125
            C2 = 2 * float(np.pi) - C1
            MAGIC = 1.5 * 2.0 ** 23
            for l in range(2):
                dve.wait_ge(filt_in, 16 * 5)
                dve.wait_ge(f_mm, l + 1)
                if l:
                    dve.wait_ge(f_sin, l)
                a, n = farg[0:64, :], fturn[0:64, :]
                chain.link(nc.vector.tensor_scalar(a, bank[6][0:64, 0:T], fcol[0:64, 2 * l:2 * l + 1], fcol[0:64, 2 * l + 1:2 * l + 2],
                                                   ALU.add, ALU.mult))
                chain.link(nc.vector.tensor_scalar(n, a, 1.0 / (2 * float(np.pi)), MAGIC, ALU.mult, ALU.add))
                chain.link(nc.vector.tensor_scalar(n, n, MAGIC, None, ALU.subtract))
                chain.link(nc.vector.scalar_tensor_tensor(out=a, in0=n, scalar=-C1, in1=a, op0=ALU.mult, op1=ALU.add))
                chain.link(nc.vector.scalar_tensor_tensor(out=a, in0=n, scalar=-C2, in1=a, op0=ALU.mult, op1=ALU.add))
                nc.vector.tensor_scalar(a, a, -3.1415925, 3.1415925, ALU.max, ALU.min).then_inc(f_lin, 1)
                if l == 0:
                    dve.wait_ge(x_in, 48)
                    nc.vector.tensor_tensor(X[:, :, 0:T], X[:, :, 0:T], pos, ALU.add).then_inc(x_ready, 1)
                    dve.wait_ge(x_ready, 1)
            norm_dve(dve, chain, T2)
            dve.wait_ge(vecs_in, 32)
            lbv = vec("lb").rearrange("p (l n) -> p l n", l=2)
            chain.link(nc.vector.tensor_tensor(lbc, lbv[:, 0, :], lbv[:, 1, :], ALU.max))
            nc.vector.tensor_tensor(lbt, lbv, bc(lbc.unsqueeze(1), [P, 2, 8]), ALU.subtract).then_inc(lb_e, 1)
            dve.wait_ge(taps_in, 32)
            for t in range(TT):
                for j in range(2):
                    dve.wait_ge(f_mm, 3 + 2 * t + j)
                    nc.vector.tensor_tensor(hfilt[:, t, j, :], bank[2 * t + j][:], decay[:, t, :], ALU.mult).then_inc(f_taps, 1)
            for m in range(N_MOD_1):
                mod_step_dve(dve, m)
            dve.wait_ge(mcol_out, N_MOD_1)
            coef_dve(chain, vec("n1g"), mod1, 8, True)
            modulate_dve(dve, True)
            dve.wait_ge(lb_ready, 1)
            chain.link(nc.vector.tensor_tensor(lbc, lbt[:, 0, :], lbt[:, 1, :], ALU.add))
            chain.link(nc.vector.reciprocal(lbc, lbc))
            chain.link(nc.vector.tensor_tensor(omlb, lbt[:, 1, :], lbc, ALU.mult))
            chain.link(nc.vector.tensor_tensor(lbc, lbt[:, 0, :], lbc, ALU.mult))

        ar.to(m_first)
        sg = ar.take(2, 2, H1, T)
        sn = ar.take(2, 2, H1, T)
        qT = ar.take(H1, T)
        vN = ar.take(4, H1 * DK)
        gS = ar.take(H1, T)
        m_gla = ar.mark()
        proj_mm, proj_out = sem("proj_mm"), sem("proj_out")
        projected = [0, 0]
        NB = 4

        def proj_tile(pe, c, j, rhs, n, last, kt=DT, weight=slot_k):
            i = projected[0]
            projected[0] += 1
            if i >= NB:
                pe.wait_ge(proj_out, i - NB + 1)
            for k in range(kt):
                mm = nc.tensor.matmul(bank[i % NB][:, 0:n], weight(c, k, j * P, (j + 1) * P), rhs(k), start=(k == 0), stop=(k == kt - 1))
            mm.then_inc(proj_mm, 1)
            if last:
                last_use[c] = (proj_mm, i + 1)

        def proj_first(pe, c, rhs, n, modulated, extra=None):
            i = projected[0]
            projected[0] += 4
            pe.wait_ge(proj_out, i)
            chunk_wait(pe, c)
            for k in range(DT):
                pe.wait_ge(hmod, modulated(k))
                if extra is not None:
                    extra(k)
                for j in range(4):
                    mm = nc.tensor.matmul(bank[(i + j) % NB][:, 0:n], slot_k(c, k, j * P, (j + 1) * P), rhs(k), start=(k == 0), stop=(k == DT - 1))
                    if k == DT - 1:
                        mm.then_inc(proj_mm, 1)
            last_use[c] = (proj_mm, i + 4)

        def proj_rows(pe, c, t, last):
            i = projected[0]
            projected[0] += 1
            if i >= NB:
                pe.wait_ge(proj_out, i - NB + 1)
            for k in range(DT):
                mm = nc.tensor.matmul(bank[i % NB][:], H[:, k, t * P:(t + 1) * P], slot_k(c, k, 0, 512), start=(k == 0), stop=(k == DT - 1))
            mm.then_inc(proj_mm, 1)
            if last:
                last_use[c] = (proj_mm, i + 1)

        def next_tile(eng):
            i = projected[1]
            projected[1] += 1
            eng.wait_ge(proj_mm, i + 1)
            return bank[i % NB]

        def h_all(k):
            return H[:, k, :]

        def h_x(k):
            return H[:, k, 0:T]

        def in1_pe(pe):
            m = N_MOD_1
            for c, kind in ((0, "q"), (1, "z"), (2, "z"), (3, "v"), (4, "g")):
                chunk_wait(pe, in_chunk[c])
                for j in range(max(4, HOSTED[c])):
                    if j >= 4:
                        pass
                    elif kind == "v":
                        proj_rows(pe, in_chunk[c], j, j == 3)
                    elif kind == "z":
                        proj_tile(pe, in_chunk[c], j, h_all, T2, j == 3)
                    else:
                        proj_tile(pe, in_chunk[c], j, h_x, T, j == 3)
                    if j < HOSTED[c]:
                        if m > N_MOD_1:
                            mod_cols_pe(pe, m - 1)
                        mod_rows_pe(pe, m)
                        m += 1
            mod_cols_pe(pe, N_MOD_2 - 1)

        def in1_act(act, chain):
            for j in range(4):
                b = next_tile(act)
                nc.scalar.copy(qT[:, j, :], b[:, 0:T]).then_inc(proj_out, 1)
            for dr in range(2):
                for j in range(4):
                    b = next_tile(act)[:].rearrange("p (s t) -> p s t", s=2)
                    nc.scalar.activation(sg[:, :, dr, j, :], b, ACT.Sigmoid)
                    nc.scalar.activation(sn[:, :, dr, j, :], b, ACT.Sigmoid, scale=-1.0).then_inc(proj_out, 1)
            for t in range(4):
                b = next_tile(act)
                nc.scalar.copy(vN[:, t, :], b[:]).then_inc(proj_out, 1)
            for j in range(4):
                b = next_tile(act)
                nc.scalar.activation(gS[:, j, :], b[:, 0:T], ACT.Silu).then_inc(proj_out, 1)
            act.wait_ge(small_in, N_SMALL)

        def in1_dve(dve, chain):
            for m in range(N_MOD_1, N_MOD_2):
                mod_step_dve(dve, m)

        cum = ar.take(2, 2, H1, T)
        ctx_rows = ar.take(2, TT, H1 * DK)
        ge = ar.take(2, 3, H1 * T)
        etot = ar.take(2, H1 * NCH)
        st_all = ar.take(2, 2, H1, DK)
        chunk_mask, whole_mask = ge[:, 0, 0, :], ge[:, 0, 1, :]
        m_ya = ar.mark()
        yaT = ar.take(H1, T)
        gmask_f = ar.take(2, P)
        gla_mask = gmask_f.bitcast(I32)
        kd_rows = sg[:, 0, :, :, :].rearrange("p a h t -> p (a h t)").rearrange("p (d t n) -> p d t n", d=2, t=TT)
        sc = sg[:, 1, :, :, :].rearrange("p a h t -> p (a h t)").rearrange("p (d t n) -> p d t n", d=2, t=TT)
        dif = ctx_rows.rearrange("p d t n -> p d (t n)")
        logf_done, ctx_dec, ctxT_mm, ctxT_out, s0_mm = (sem("logf_done"), sem("ctx_dec"), sem("ctxT_mm"), sem("ctxT_out"), sem("s0_mm"))
        dif_done, exp_done, gq_done, kdT_mm, kdT_out, sc_mm, sc_out = (sem("dif_done"), sem("exp_done"), sem("gq_done"), sem("kdT_mm"), sem("kdT_out"), sem("sc_mm"), sem("sc_out"))
        st_ready, delta_mm, inter_mm, osq_done, osum_mm, ostd_done, mask_in = (sem("st_ready"), sem("delta_mm"), sem("inter_mm"), sem("osq_done"), sem("osum_mm"), sem("ostd_done"), sem("mask_in"))

        def flat3(ap):
            return ap.rearrange("p h t -> p (h t)")

        def gla_pe(pe):
            for m in range(N_MOD_2, N_MOD):
                mod_rows_pe(pe, m)
                mod_cols_pe(pe, m)
            n = 0
            for dr in range(2):
                for t in range(TT):
                    pe.wait_ge(ctx_dec, dr + 1)
                    for h in range(H1):
                        mm = nc.tensor.transpose(bank[n % 4][:, h * P:(h + 1) * P], cum[:, 1, dr, h, t * P:(t + 1) * P], ident[:])
                    mm.then_inc(ctxT_mm, 1)
                    n += 1
            pe.wait_ge(ctxT_out, 4)
            for dr in range(2):
                for h in range(H1):
                    for t in range(TT):
                        mm = nc.tensor.matmul(bank[4 + dr][:, h * P:(h + 1) * P], ctx_rows[:, dr, t, h * P:(h + 1) * P],
                                              vN[:, 2 + t, h * P:(h + 1) * P], start=(t == 0), stop=(t == 1), skip_group_check=True)
            mm.then_inc(s0_mm, 1)
            n = 0
            for dr in range(2):
                pe.wait_ge(gq_done, 3 * dr + 2)
                for t in range(TT):
                    for h in range(H1):
                        s = slice(h * T + t * P, h * T + (t + 1) * P)
                        mm = nc.tensor.matmul(bank[n][:, h * P:(h + 1) * P], ge[:, dr, 1, s], ge[:, dr, 0, s], start=True, stop=True,
                                              skip_group_check=True)
                    mm.then_inc(sc_mm, 1)
                    n += 1
            pe.wait_ge(st_ready, 1)
            n = 0
            for dr in range(2):
                pe.wait_ge(gq_done, 3 * dr + 3)
                for t in range(TT):
                    if n == 2:
                        pe.wait_ge(kdT_out, 2)
                    for h in range(H1):
                        s = slice(h * T + t * P, h * T + (t + 1) * P)
                        mm = nc.tensor.transpose(bank[4 + n % 2][:, h * P:(h + 1) * P], ge[:, dr, 2, s], ident[:])
                    mm.then_inc(kdT_mm, 1)
                    n += 1
            pe.wait_ge(sc_out, 4)
            for h in range(H1):
                for t in range(TT):
                    for dr in range(2):
                        o = bank[6 + h // 2][:, (h % 2) * T + t * P:(h % 2) * T + (t + 1) * P]
                        nc.tensor.matmul(o, vN[:, t, h * P:(h + 1) * P], sc[:, dr, t, h * P:(h + 1) * P],
                                         start=(h % 2 + t + dr == 0), stop=False, skip_group_check=True)
            pe.wait_ge(kdT_out, 4)
            for i in range(NCH):
                if i >= 2:
                    pe.wait_ge(st_ready, 2 * i - 1)
                for dr in range(2):
                    cidx = i if dr == 0 else NCH - 1 - i
                    t, r = cidx // 4, 32 * (cidx % 4)
                    if i < NCH - 1:
                        for h in range(H1):
                            mm = nc.tensor.matmul(bank[2 * (i % 2) + dr][:, h * P:(h + 1) * P], kd_rows[r:r + 32, dr, t, h * P:(h + 1) * P],
                                                  vN[r:r + 32, t, h * P:(h + 1) * P], start=True, stop=True, skip_group_check=True)
                        mm.then_inc(delta_mm, 1)
                if i >= 1:
                    pe.wait_ge(st_ready, 1 + 2 * i)
                for dr in range(2):
                    cidx = i if dr == 0 else NCH - 1 - i
                    for h in range(H1):
                        c0 = (h % 2) * T + cidx * CHUNK
                        mm = nc.tensor.matmul(bank[6 + h // 2][:, c0:c0 + CHUNK], st_all[:, i % 2, dr, h, :],
                                              cum[:, 0, dr, h, cidx * CHUNK:(cidx + 1) * CHUNK], start=False, stop=(i == NCH - 1),
                                              skip_group_check=True)
                mm.then_inc(inter_mm, 1)
            for b in range(2):
                pe.wait_ge(osq_done, b + 1)
                nc.tensor.matmul(bank[4 + b][:], ones[:], dif[:, 0, b * 512:(b + 1) * 512], start=True, stop=True).then_inc(osum_mm, 1)
            chunk_wait(pe, in_chunk[5])
            for j in range(4):
                proj_tile(pe, in_chunk[5], j, h_x, T, j == 3)

        def gla_act(act, chain):
            act.dma_start(gmask_f, d["gla_mask"].bitcast(F32)).then_inc(mask_in, 16)
            for dr in range(2):
                for h in range(H1):
                    n = dr * H1 + h
                    nc.scalar.activation(sg[:, :, dr, h, :], sg[:, :, dr, h, :], ACT.Ln, bias=lbc[:, n:n + 1],
                                         scale=omlb[:, n:n + 1]).then_inc(logf_done, 1)
            for dr in range(2):
                act.wait_ge(dif_done, dr + 1)
                nc.scalar.activation(cum[:, 1, dr, :, :], cum[:, 1, dr, :, :], ACT.Exp).then_inc(exp_done, 1)
            n = 0
            for dr in range(2):
                for t in range(TT):
                    n += 1
                    act.wait_ge(ctxT_mm, n)
                    nc.scalar.copy(ctx_rows[:, dr, t, :], bank[(n - 1) % 4][:]).then_inc(ctxT_out, 1)
            act.wait_ge(s0_mm, 1)
            for dr in range(2):
                ins = nc.scalar.copy(st_all[:, 0, dr, :, :].rearrange("p h v -> p (h v)"), bank[4 + dr][:])
            ins.then_inc(st_ready, 1)
            for dr in range(2):
                act.wait_ge(dif_done, 3 + 2 * dr)
                nc.scalar.activation(ge[:, dr, 0, :], dif[:, dr, :], ACT.Exp)
                nc.scalar.activation(ge[:, dr, 1, :], dif[:, dr, :], ACT.Exp, scale=-1.0).then_inc(exp_done, 1)
                act.wait_ge(dif_done, 4 + 2 * dr)
                nc.scalar.activation(ge[:, dr, 2, :], ge[:, dr, 2, :], ACT.Exp)
                nc.scalar.activation(cum[:, 0, dr, :, :], cum[:, 0, dr, :, :], ACT.Exp).then_inc(exp_done, 1)
            n = 0
            for dr in range(2):
                for t in range(TT):
                    n += 1
                    act.wait_ge(kdT_mm, n)
                    nc.scalar.copy(kd_rows[:, dr, t, :], bank[4 + (n - 1) % 2][:]).then_inc(kdT_out, 1)
            act.wait_ge(inter_mm, NCH)
            for b in range(2):
                nc.scalar.activation(dif[:, 0, b * 512:(b + 1) * 512], bank[6 + b][:], ACT.Square).then_inc(osq_done, 1)
            for b in range(2):
                act.wait_ge(osum_mm, b + 1)
                nc.scalar.activation(dif[:, 1, b * 512:(b + 1) * 512], bank[4 + b][:], ACT.Sqrt, bias=epsc[:], scale=1.0 / DK).then_inc(ostd_done, 1)

        def gla_dve(dve, chain):
            chain.link(nc.vector.memset(chunk_mask, 1.0))
            chain.link(nc.vector.memset(chunk_mask.rearrange("p (c s) -> p c s", s=CHUNK)[:, :, 0:1], 0.0))
            chain.link(nc.vector.memset(whole_mask, 1.0))
            chain.link(nc.vector.memset(whole_mask.rearrange("p (c s) -> p c s", s=T)[:, :, 0:1], 0.0))
            for dr in range(2):
                for h in range(H1):
                    n = dr * H1 + h
                    ins = nc.vector.tensor_scalar(sn[:, :, dr, h, :], sn[:, :, dr, h, :], omlb[:, n:n + 1], None, ALU.mult)
                    if n % 2:
                        mod_step_dve(dve, N_MOD_2 + n // 2)
            chain.link(ins)
            for dr in range(2):
                dve.wait_ge(logf_done, H1 * (dr + 1))
                lf, cu = flat3(sg[:, 1, dr, :, :]), flat3(cum[:, 1, dr, :, :])
                step = -1 if dr == 0 else 1
                chain.link(nc.vector.tensor_tensor_scan(cu[:, ::step], whole_mask, lf[:, ::step], 0.0, ALU.mult, ALU.add))
                nc.vector.tensor_tensor(cu, cu, lf, ALU.subtract).then_inc(dif_done, 1)
            mod_step_dve(dve, N_MOD - 1)
            for dr in range(2):
                lf, cu = flat3(sg[:, 0, dr, :, :]), flat3(cum[:, 0, dr, :, :])
                step = 1 if dr == 0 else -1
                chain.link(nc.vector.tensor_tensor_scan(cu[:, ::step], chunk_mask, lf[:, ::step], 0.0, ALU.mult, ALU.add))
            for dr in range(2):
                dve.wait_ge(exp_done, dr + 1)
                nc.vector.tensor_tensor(cum[:, 1, dr, :, :], cum[:, 1, dr, :, :], sn[:, 1, dr, :, :], ALU.mult).then_inc(ctx_dec, 1)
            dve.wait_ge(s0_mm, 1)
            for dr in range(2):
                b3 = flat3(cum[:, 0, dr, :, :]).rearrange("p (c s) -> p c s", s=CHUNK)
                ref = CHUNK // 2 if dr == 0 else CHUNK - 1 - CHUNK // 2
                end = CHUNK - 1 if dr == 0 else 0
                shape = [P, H1 * NCH, CHUNK]
                nc.vector.tensor_tensor(dif[:, dr, :].rearrange("p (c s) -> p c s", s=CHUNK), b3, bc(b3[:, :, ref:ref + 1], shape),
                                        ALU.subtract).then_inc(dif_done, 1)
                nc.vector.tensor_tensor(ge[:, dr, 2, :].rearrange("p (c s) -> p c s", s=CHUNK), bc(b3[:, :, end:end + 1], shape), b3,
                                        ALU.subtract).then_inc(dif_done, 1)
            for dr in range(2):
                q2, k2 = flat3(qT), flat3(sn[:, 0, dr, :, :])
                dve.wait_ge(exp_done, 3 + 2 * dr)
                nc.vector.tensor_tensor(ge[:, dr, 0, :], ge[:, dr, 0, :], q2, ALU.mult).then_inc(gq_done, 1)
                nc.vector.tensor_tensor(ge[:, dr, 1, :], ge[:, dr, 1, :], k2, ALU.mult).then_inc(gq_done, 1)
                dve.wait_ge(exp_done, 4 + 2 * dr)
                c2 = flat3(cum[:, 0, dr, :, :])
                end = CHUNK - 1 if dr == 0 else 0
                chain.link(nc.vector.tensor_copy(etot[:, dr, :], c2.rearrange("p (c s) -> p c s", s=CHUNK)[:, :, end]))
                chain.link(nc.vector.tensor_tensor(c2, c2, q2, ALU.mult))
                nc.vector.tensor_tensor(ge[:, dr, 2, :], ge[:, dr, 2, :], k2, ALU.mult).then_inc(gq_done, 1)
            dve.wait_ge(mask_in, 16)
            chain.link(nc.vector.memset(sc, 0.0))
            n = 0
            for dr in range(2):
                for t in range(TT):
                    n += 1
                    dve.wait_ge(sc_mm, n)
                    nc.vector.copy_predicated(sc[:, dr, t, :].rearrange("p (h t) -> p h t", h=H1),
                                              bc(gla_mask[:, dr, :].unsqueeze(1), [P, H1, P]),
                                              bank[n - 1][:].rearrange("p (h t) -> p h t", h=H1)).then_inc(sc_out, 1)
            dve.wait_ge(st_ready, 1)
            for i in range(NCH - 1):
                for dr in range(2):
                    cidx = i if dr == 0 else NCH - 1 - i
                    dve.wait_ge(delta_mm, 2 * i + dr + 1)
                    if i >= 1:
                        dve.wait_ge(inter_mm, i)
                        dve.wait_ge(st_ready, 1 + 2 * i)
                    for h in range(H1):
                        ins = nc.vector.scalar_tensor_tensor(out=st_all[:, (i + 1) % 2, dr, h, :], in0=st_all[:, i % 2, dr, h, :],
                                                             scalar=etot[:, dr, h * NCH + cidx:h * NCH + cidx + 1],
                                                             in1=bank[2 * (i % 2) + dr][:, h * P:(h + 1) * P], op0=ALU.mult, op1=ALU.add)
                    ins.then_inc(st_ready, 1)
            for b in range(2):
                dve.wait_ge(ostd_done, b + 1)
                r = dif[:, 1, b * 512:(b + 1) * 512]
                y = flat3(yaT)[:, b * 512:(b + 1) * 512]
                chain.link(nc.vector.reciprocal(r, r))
                chain.link(nc.vector.scalar_tensor_tensor(out=y, in0=bank[6 + b][:], scalar=vec("hng"), in1=r, op0=ALU.mult, op1=ALU.mult))
                chain.link(nc.vector.tensor_tensor(y, y, flat3(gS)[:, b * 512:(b + 1) * 512], ALU.mult))


        ar.to(m_first)
        ybT = ar.take(4, T)
        hyp = ar.take(12, T + 2)
        hyu = ar.take(12, T)
        assert ar.at <= m_gla
        ar.to(m_gla)
        un = ar.take(TT, HYW)
        uf = ar.take(4, HYW)
        ys = ar.take(4, HYW)
        ytmp = ar.take(HYW)
        conv_done, uT_mm, uT_out, u_mm, u_out, ys_done, y_mm = (sem("conv_done"), sem("uT_mm"), sem("uT_out"), sem("u_mm"), sem("u_out"), sem("ys_done"), sem("y_mm"))
        vx_done = sem("vx_done")

        def hy_pe(pe):
            for c in (6, 7):
                chunk_wait(pe, in_chunk[c])
                for j in range(4):
                    proj_tile(pe, in_chunk[c], j, h_x, T, j == 3)
            pe.wait_ge(vx_done, 4)
            for t in range(TT):
                for j in range(4):
                    mm = nc.tensor.transpose(bank[4 + t][:, j * P:(j + 1) * P], hyu[:, j, t * P:(t + 1) * P], ident[:])
                mm.then_inc(uT_mm, 1)
            for m in range(4):
                pe.wait_ge(uT_out, 2)
                if m >= 2:
                    pe.wait_ge(u_out, m - 1)
                for t in range(TT):
                    mm = nc.tensor.matmul(bank[6 + m % 2][:], dft_u[:, t, m * P:(m + 1) * P], un[:, t, :], start=(t == 0), stop=(t == 1))
                mm.then_inc(u_mm, 1)
            chunk_wait(pe, in_chunk[8])
            for j in range(4):
                proj_tile(pe, in_chunk[8], j, h_x, T, j == 3)
            pe.wait_ge(ys_done, 4)
            for j in range(4):
                for m in range(4):
                    mm = nc.tensor.matmul(bank[4 + j][:, 0:T], ys[:, m, j * P:(j + 1) * P], idft[:, m, :],
                                          start=(m == 0), stop=(m == 3), skip_group_check=True)
                mm.then_inc(y_mm, 1)

        def hy_act(act, chain):
            for n in range(12):
                b = next_tile(act)
                if n == 0:
                    act.wait_ge(conv_done, 1)
                nc.scalar.copy(hyp[:, n, 1:T + 1], b[:, 0:T]).then_inc(proj_out, 1)
            for t in range(TT):
                act.wait_ge(uT_mm, t + 1)
                nc.scalar.copy(un[:, t, :], bank[4 + t][:]).then_inc(uT_out, 1)
            for m in range(4):
                act.wait_ge(u_mm, m + 1)
                nc.scalar.copy(uf[:, m, :], bank[6 + m % 2][:]).then_inc(u_out, 1)

        def hy_dve(dve, chain):
            nc.vector.memset(hyp, 0.0).then_inc(conv_done, 1)
            for n in range(12):
                dve.wait_ge(proj_out, 20 + n + 1)
                u = hyu[:, n, :]
                chain.link(nc.vector.tensor_scalar(u, hyp[:, n, 0:T], vec("cw", n, n + 1), vec("cb", n, n + 1), ALU.mult, ALU.add))
                chain.link(nc.vector.scalar_tensor_tensor(out=u, in0=hyp[:, n, 1:T + 1], scalar=vec("cw", 12 + n, 13 + n), in1=u, op0=ALU.mult, op1=ALU.add))
                chain.link(nc.vector.scalar_tensor_tensor(out=u, in0=hyp[:, n, 2:T + 2], scalar=vec("cw", 24 + n, 25 + n), in1=u, op0=ALU.mult, op1=ALU.add))
                if 4 <= n < 8:
                    nc.vector.tensor_tensor(hyu[:, n - 4, :], hyu[:, n - 4, :], u, ALU.mult).then_inc(vx_done, 1)
            dve.wait_ge(u_out, 4)
            for b in range(2):
                tmp = ytmp
                re, im = uf[:, b, :], uf[:, 2 + b, :]
                chain.link(nc.vector.tensor_tensor(ys[:, b, :], re, hyk[:, b, :], ALU.mult))
                chain.link(nc.vector.tensor_tensor(tmp, im, hyk[:, 2 + b, :], ALU.mult))
                nc.vector.tensor_tensor(ys[:, b, :], ys[:, b, :], tmp, ALU.subtract).then_inc(ys_done, 1)
                chain.link(nc.vector.tensor_tensor(ys[:, 2 + b, :], re, hyk[:, 2 + b, :], ALU.mult))
                chain.link(nc.vector.tensor_tensor(tmp, im, hyk[:, 4 if b == 0 else 1, :], ALU.mult))
                nc.vector.tensor_tensor(ys[:, 2 + b, :], ys[:, 2 + b, :], tmp, ALU.add).then_inc(ys_done, 1)
            for j in range(4):
                dve.wait_ge(y_mm, j + 1)
                y = bank[4 + j][:, 0:T]
                chain.link(nc.vector.scalar_tensor_tensor(out=ybT[:, j, :], in0=hyu[:, j, :], scalar=vec("hyd", j, j + 1), in1=y, op0=ALU.mult, op1=ALU.add))
                chain.link(nc.vector.tensor_tensor(ybT[:, j, :], ybT[:, j, :], hyu[:, 8 + j, :], ALU.mult))

        ga = ar.take(2, DT, T)
        mix = ar.take(DT, T)
        mtmp = ar.take(2, T)
        assert ar.at <= m_ya
        mg_mm, mix_done, wo_mm, x1_done = sem("mg_mm"), sem("mix_done"), sem("wo_mm"), sem("x1_done")

        def merge_pe(pe):
            for c in (9, 10, 11):
                chunk_wait(pe, in_chunk[c])
                for j in range(4):
                    proj_tile(pe, in_chunk[c], j, h_x, T, j == 3)
            ca, cb = pa_chunk, pb_chunk
            chunk_wait(pe, ca)
            chunk_wait(pe, cb)
            for j in range(DT):
                if j >= 2:
                    pe.wait_ge(mix_done, j - 1)
                for half, (c, y) in enumerate(((ca, yaT), (cb, ybT))):
                    for k in range(4):
                        mm = nc.tensor.matmul(bank[4 + j % 2][:, half * T:(half + 1) * T], slot_w(c, k, j * P, (j + 1) * P), y[:, k, :],
                                              start=(k == 0), stop=(k == 3), skip_group_check=True)
                mm.then_inc(mg_mm, 1)
            last_use[ca] = last_use[cb] = (mg_mm, DT)
            for j in range(DT):
                c = out_chunk[j // 4]
                chunk_wait(pe, c)
                if j == 0:
                    pe.wait_ge(mix_done, DT)
                if j >= 2:
                    pe.wait_ge(x1_done, j - 1)
                for k in range(DT):
                    mm = nc.tensor.matmul(bank[6 + j % 2][:, 0:T], slot_k(c, k, (j % 4) * P, (j % 4 + 1) * P), mix[:, k, :],
                                          start=(k == 0), stop=(k == DT - 1))
                mm.then_inc(wo_mm, 1)
                if j % 4 == 3:
                    last_use[c] = (wo_mm, j + 1)
            pe.wait_ge(x1_done, DT)
            norm_pe(pe, H, T)

        def merge_act(act, chain):
            for n in range(16):
                b = next_tile(act)
                nc.scalar.activation(ga[:, n // 8, n % 8, :], b[:, 0:T], ACT.Sigmoid).then_inc(proj_out, 1)
            for k in range(DT):
                act.wait_ge(x1_done, k + 1)
                nc.scalar.activation(H[:, k, 0:T], X[:, k, 0:T], ACT.Square).then_inc(sq_ready, 1)
            std_act(act, T)

        def merge_dve(dve, chain):
            dve.wait_ge(proj_out, 20 + 12 + 16)
            for j in range(DT):
                dve.wait_ge(mg_mm, j + 1)
                b = bank[4 + j % 2]
                nc.vector.tensor_tensor(mtmp[:, 0, :], ga[:, 0, j, :], b[:, 0:T], ALU.mult)
                chain.link(nc.vector.tensor_tensor(mtmp[:, 1, :], ga[:, 1, j, :], b[:, T:T2], ALU.mult))
                ins = nc.vector.tensor_tensor(mix[:, j, :], mtmp[:, 0, :], mtmp[:, 1, :], ALU.add)
                ins.then_inc(mix_done, 1)
                dve.wait_ge(mix_done, j + 1)
            for j in range(DT):
                dve.wait_ge(wo_mm, j + 1)
                nc.vector.scalar_tensor_tensor(out=X[:, j, 0:T], in0=bank[6 + j % 2][:, 0:T], scalar=mod1[:, 16 + j, 0:1],
                                               in1=X[:, j, 0:T], op0=ALU.mult, op1=ALU.add).then_inc(x1_done, 1)

        ar.to(0)
        comb = ar.take(TT, NG * NE)
        acc = ar.take(TT, D)
        hrows = ar.take(TT, D)
        place = ar.take(TT, NX + 2)
        slot_no = ar.take(CAP)
        over = ar.take(1).bitcast(I32)
        m_moe = ar.mark()
        tri = ar.take(P)
        member = ar.take(TT, NX)
        count = ar.take(1)
        lg = ar.take(TT, 36)
        r1, r2, r3, r4 = ar.take(TT, 1), ar.take(TT, 1), ar.take(TT, 1), ar.take(TT, 1)
        eq4, key4, oh4, ex4 = ar.take(TT, 4), ar.take(TT, 4), ar.take(TT, 4), ar.take(TT, 4)
        el, eq8, key8, oh1, oh2, tm8 = (ar.take(TT, 8) for _ in range(6))
        ctx2_in, rt_mm, rt_x, rt_e = sem("ctx2_in"), sem("rt_mm"), sem("rt_x"), sem("rt_e")
        tables_in, hrow_mm, member_out, place_mm = sem("tables_in"), sem("hrow_mm"), sem("member_out"), sem("place_mm")

        def router_pe(pe):
            for k in range(DT):
                pe.wait_ge(hmod, 2 * DT + k + 1)
            for t in range(TT):
                for k in range(DT):
                    mm = nc.tensor.matmul(bank[t][:, 0:36], H[:, k, t * P:(t + 1) * P], router_w[:, k, :], start=(k == 0), stop=(k == DT - 1))
                mm.then_inc(rt_mm, 1)
            for t in range(TT):
                for k in range(DT):
                    mm = nc.tensor.transpose(bank[2 + 2 * t + k // 4][:, (k % 4) * P:(k % 4 + 1) * P], H[:, k, t * P:(t + 1) * P], ident[:])
                    if k % 4 == 3:
                        mm.then_inc(hrow_mm, 1)
            pe.wait_ge(tables_in, 32)
            pe.wait_ge(member_out, 1)
            nc.tensor.matmul(bank[0][:, 0:NX], tri, member[:, 0, :], start=True, stop=True)
            nc.tensor.matmul(bank[0][:, NX:2 * NX], ones[:], member[:, 0, :], start=True, stop=False, skip_group_check=True)
            nc.tensor.matmul(bank[0][:, NX:2 * NX], tri, member[:, 1, :], start=False, stop=True, skip_group_check=True)
            nc.tensor.matmul(bank[1][:, 0:NX], ones[:], member[:, 0, :], start=True, stop=False)
            nc.tensor.matmul(bank[1][:, 0:NX], ones[:], member[:, 1, :], start=False, stop=True).then_inc(place_mm, 1)

        def router_act(act, chain):
            act.dma_start(tri, d["tri"]).then_inc(tables_in, 16)
            act.dma_start(slot_no, d["slot_no"]).then_inc(tables_in, 16)
            act.dma_start(X[:, :, T:T2], d["ctx_2"]).then_inc(ctx2_in, 16)
            modulate_act(act, mod1, 24, False)
            for n in range(4):
                act.wait_ge(hrow_mm, n + 1)
                nc.scalar.copy(hrows[:, n // 2, (n % 2) * 512:(n % 2 + 1) * 512], bank[2 + n][:])
            act.wait_ge(rt_x, 1)
            nc.scalar.activation(ex4, ex4, ACT.Exp).then_inc(rt_e, 1)
            act.wait_ge(rt_x, 2)
            nc.scalar.activation(r3, r3, ACT.Exp).then_inc(rt_e, 1)
            act.wait_ge(ctx2_in, 16)

        def router_dve(dve, chain):
            L = chain.link
            V = nc.vector
            norm_dve(dve, chain, T)
            coef_dve(chain, vec("n2g"), mod1, 32, False)
            modulate_dve(dve, False)
            for t in range(TT):
                dve.wait_ge(rt_mm, t + 1)
                L(V.tensor_tensor(lg[:, t, :], bank[t][:, 0:36], router_b[:], ALU.add))
            s4, s8 = [P, TT, 4], [P, TT, 8]

            def first_max(x, shape, mx, eq, key, hot):
                L(V.tensor_reduce(mx[:, :, 0], x, AXX, ALU.max))
                L(V.tensor_tensor(eq, x, bc(mx, shape), ALU.is_equal))
                L(V.tensor_tensor(key, eq, bc(tie[:, 0:shape[2]].unsqueeze(1), shape), ALU.mult))
                L(V.tensor_reduce(r4[:, :, 0], key, AXX, ALU.max))
                L(V.tensor_tensor(hot, key, bc(r4, shape), ALU.is_equal))

            g4 = lg[:, :, 0:4]
            first_max(g4, s4, r1, eq4, key4, oh4)
            V.tensor_tensor(ex4, g4, bc(r1, s4), ALU.subtract).then_inc(rt_x, 1)
            dve.wait_ge(rt_e, 1)
            L(V.tensor_reduce(r2[:, :, 0], ex4, AXX, ALU.add))
            L(V.reciprocal(r2, r2))
            for g in range(NG):
                dst = el if g == 0 else tm8
                L(V.tensor_tensor(dst, lg[:, :, 4 + 8 * g:12 + 8 * g], bc(oh4[:, :, g:g + 1], s8), ALU.mult))
                if g:
                    L(V.tensor_tensor(el, el, tm8, ALU.add))
            first_max(el, s8, r1, eq8, key8, oh1)
            L(V.tensor_scalar(tm8, oh1, -BIG, None, ALU.mult))
            L(V.tensor_tensor(el, el, tm8, ALU.add))
            L(V.tensor_copy(r3, r1))
            first_max(el, s8, r1, eq8, key8, oh2)
            V.tensor_tensor(r3, r1, r3, ALU.subtract).then_inc(rt_x, 1)
            L(V.tensor_tensor(tm8, oh1, oh2, ALU.add))
            for g in range(NG):
                ins = V.tensor_tensor(member[:, :, g * NE:(g + 1) * NE], tm8, bc(oh4[:, :, g:g + 1], s8), ALU.mult)
            ins.then_inc(member_out, 1)
            dve.wait_ge(rt_e, 2)
            L(V.tensor_scalar(r1, r3, 1.0, None, ALU.add))
            L(V.reciprocal(r1, r1))
            L(V.tensor_tensor(r2, r2, r1, ALU.mult))
            L(V.tensor_tensor(r3, r2, r3, ALU.mult))
            L(V.tensor_tensor(oh1, oh1, bc(r2, s8), ALU.mult))
            L(V.tensor_tensor(oh2, oh2, bc(r3, s8), ALU.mult))
            L(V.tensor_tensor(oh1, oh1, oh2, ALU.add))
            for g in range(NG):
                L(V.tensor_tensor(comb[:, :, g * NE:(g + 1) * NE], oh1, bc(oh4[:, :, g:g + 1], s8), ALU.mult))
            L(V.memset(place, -1.0))
            dve.wait_ge(place_mm, 1)
            L(V.tensor_tensor(place[:, :, 0:NX], bank[0][:, 0:2 * NX].rearrange("p (t e) -> p t e", e=NX), member, ALU.mult))
            L(V.tensor_scalar(place[:, :, 0:NX], place[:, :, 0:NX], -1.0, None, ALU.add))
            L(V.tensor_reduce(count, bank[1][:, 0:NX], AXX, ALU.max))
            L(V.tensor_scalar(over, count, float(CAP), None, ALU.is_gt))

        ar.to(m_moe)
        moe_ring_free = sem("moe_ring_free")
        wg, wu, wd = d["moe_w_gate"], d["moe_w_up"], d["moe_w_down"]
        NPAIR = NX // 2
        gath = ar.take(DT, P)
        pick = ar.take(TT, P)
        pick_w = ar.take(TT, P)
        pick_t = ar.take(TT, P)
        psig = ar.take(512)
        phid = ar.take(512)
        phid_t = ar.take(4, P)
        py = ar.take(D)
        extra = work[:, WORK - 3 * SLOT:WORK].rearrange("p (s w) -> p s w", w=SLOT)
        pair_slot = [ring[:, s, :] for s in moe_slots] + [extra[:, i, :] for i in range(3)]
        pair_in = [sem(f"pair_in{i}") for i in range(6)]
        gate_mm, up_mm, down_mm, silu_out, hid_out = sem("gate_mm"), sem("up_mm"), sem("down_mm"), sem("silu_out"), sem("hid_out")
        gath_mm, phid_mm, pick_mm, scat_mm = sem("gath_mm"), sem("phid_mm"), sem("pick_mm"), sem("scat_mm")
        gath_out, phid_t_out, pick_t_out, py_out = sem("gath_out"), sem("phid_t_out"), sem("pick_t_out"), sem("py_out")
        pick_ready, pick_w_ready = sem("pick_ready"), sem("pick_w_ready")

        def expert_src(w, e):
            s = w[e:e + 1] if isinstance(e, int) else w[bass.ds(e, 1), :, :]
            return s.rearrange("e (k p) n -> p (e k) n", p=P)

        def pair_loads(sp, p, first_time):
            for j, (w, used) in enumerate(((wg, gate_mm), (wu, up_mm), (wd, down_mm))):
                if not first_time:
                    sp.wait_ge(used, p * 2 if w is wd else p)
                for b in range(2):
                    i = 2 * j + b
                    if first_time:
                        if i < 3:
                            sp.wait_ge(*last_use[before_moe[i]])
                        else:
                            sp.wait_ge(stage_done, 3 * 5)
                    sp.dma_start(pair_slot[i].rearrange("p (k n) -> p k n", n=w.shape[2]), expert_src(w, p * 2 + b)).then_inc(pair_in[i], 16)

        def moe_sync(sp):
            pair_loads(sp, 0, True)
            sp.wait_ge(stage_done, 3 * 6)
            v = sp.value_load(over[0:1, 0:1], min_val=0, max_val=1)
            with sp.If(v == 0):
                with sp.Fori(1, NPAIR) as p:
                    pair_loads(sp, p, False)
            with sp.Else():
                for s in pair_in:
                    sp.wait_ge(s, 16)
                dense_sync(sp)

        def moe_pe(pe):
            v = pe.value_load(over[0:1, 0:1], min_val=0, max_val=1)
            with pe.If(v == 0):
                sparse_pe(pe)
            with pe.Else():
                dense_pe(pe)

        def moe_act(act, chain):
            v = act.value_load(over[0:1, 0:1], min_val=0, max_val=1)
            with act.If(v == 0):
                sparse_act(act)
            with act.Else():
                dense_act(act)

        def moe_dve(dve, chain):
            v = dve.value_load(over[0:1, 0:1], min_val=0, max_val=1)
            with dve.If(v == 0):
                sparse_dve(dve)
            with dve.Else():
                dense_dve(dve)

        def sparse_pe(pe):
            def gather(n):
                pe.wait_ge(pick_ready, n)
                for k in range(DT):
                    for t in range(TT):
                        mm = nc.tensor.matmul(bank[2 + k // 4][:, (k % 4) * P:(k % 4 + 1) * P], hrows[:, t, k * P:(k + 1) * P], pick[:, t, :],
                                              start=(t == 0), stop=(t == 1), skip_group_check=True)
                    if k % 4 == 3:
                        mm.then_inc(gath_mm, 1)

            def both(b, i, x, signal):
                for k in range(DT):
                    for e in range(2):
                        rows = slice(e * CAP, (e + 1) * CAP)
                        mm = nc.tensor.matmul(bank[b][rows, :], x[:, k, rows], pair_slot[i + e][:, k * 512:(k + 1) * 512],
                                              start=(k == 0), stop=(k == DT - 1), skip_group_check=True)
                mm.then_inc(signal, 1)

            def scatter(n, start, stop):
                pe.wait_ge(pick_t_out, n)
                pe.wait_ge(py_out, n * 2)
                for t in range(TT):
                    for half in range(2):
                        mm = nc.tensor.matmul(bank[4 + 2 * t + half][:], pick_t[:, t, :], py[:, half * 512:(half + 1) * 512],
                                              start=start, stop=stop, skip_group_check=True)
                return mm

            def pair(p, first_time, last):
                pe.wait_ge(gath_out, p * 2 + 2)
                pe.wait_ge(pair_in[0], p * 16 + 16)
                pe.wait_ge(pair_in[1], p * 16 + 16)
                both(0, 0, gath, gate_mm)
                if not first_time:
                    scatter(p, p_is_second[0], False)
                    p_is_second[0] = False
                pe.wait_ge(pair_in[2], p * 16 + 16)
                pe.wait_ge(pair_in[3], p * 16 + 16)
                both(1, 2, gath, up_mm)
                if not last:
                    gather(p + 2)
                pe.wait_ge(hid_out, p + 1)
                for f in range(4):
                    mm = nc.tensor.transpose(bank[0][:, f * P:(f + 1) * P], phid[:, f * P:(f + 1) * P], ident[:])
                mm.then_inc(phid_mm, 1)
                pe.wait_ge(pick_w_ready, p + 1)
                for t in range(TT):
                    mm = nc.tensor.transpose(bank[1][:, t * P:(t + 1) * P], pick_w[:, t, :], ident[:])
                mm.then_inc(pick_mm, 1)
                if not last:
                    pe.wait_ge(gath_out, p * 2 + 4)
                pe.wait_ge(phid_t_out, p + 1)
                pe.wait_ge(pair_in[4], p * 16 + 16)
                pe.wait_ge(pair_in[5], p * 16 + 16)
                for half in range(2):
                    for f in range(4):
                        for e in range(2):
                            rows = slice(e * CAP, (e + 1) * CAP)
                            at = f * D + half * 512
                            mm = nc.tensor.matmul(bank[2 + half][rows, :], phid_t[:, f, rows], pair_slot[4 + e][:, at:at + 512],
                                                  start=(f == 0), stop=(f == 3), skip_group_check=True)
                    mm.then_inc(down_mm, 1)

            p_is_second = [True]
            gather(1)
            pair(0, True, False)
            pair(1, False, False)
            with pe.Fori(2, NPAIR - 1) as p:
                pair(p, False, False)
            pair(NPAIR - 1, False, True)
            scatter(NPAIR, False, True).then_inc(scat_mm, 1)

        def sparse_act(act):
            def take_gathered(n):
                act.wait_ge(gath_mm, n)
                nc.scalar.copy(gath[:, 0:4, :].rearrange("p k s -> p (k s)"), bank[2][:]).then_inc(gath_out, 1)

            def pair(p, first_time, last):
                act.wait_ge(gate_mm, p + 1)
                if not first_time:
                    act.wait_ge(hid_out, p)
                nc.scalar.activation(psig, bank[0][:], ACT.Silu).then_inc(silu_out, 1)
                if not last:
                    take_gathered(p * 2 + 3)
                act.wait_ge(phid_mm, p + 1)
                nc.scalar.copy(phid_t.rearrange("p f s -> p (f s)"), bank[0][:]).then_inc(phid_t_out, 1)
                act.wait_ge(down_mm, p * 2 + 1)
                nc.scalar.copy(py[:, 0:512], bank[2][:]).then_inc(py_out, 1)

            take_gathered(1)
            pair(0, True, False)
            with act.Fori(1, NPAIR - 1) as p:
                pair(p, False, False)
            pair(NPAIR - 1, False, True)
            act.wait_ge(scat_mm, 1)
            for half in range(2):
                nc.scalar.copy(acc[:, 0, half * 512:(half + 1) * 512], bank[4 + half][:])

        def sparse_dve(dve):
            def take_gathered(n):
                dve.wait_ge(gath_mm, n)
                nc.vector.tensor_copy(gath[:, 4:8, :].rearrange("p k s -> p (k s)"), bank[3][:]).then_inc(gath_out, 1)

            def of(x, t, e):
                return x[:, t, e:e + 1] if isinstance(e, int) else x[:, t, bass.ds(e, 1)]

            def make_pick(p):
                for t in range(TT):
                    for e in range(2):
                        ins = nc.vector.tensor_scalar(pick[:, t, e * CAP:(e + 1) * CAP], slot_no, of(place, t, p * 2 + e), None, ALU.is_equal)
                ins.then_inc(pick_ready, 1)

            def make_pick_w(p):
                for t in range(TT):
                    for e in range(2):
                        ins = nc.vector.tensor_scalar(pick_w[:, t, e * CAP:(e + 1) * CAP], slot_no, of(place, t, p * 2 + e),
                                                      of(comb, t, p * 2 + e), ALU.is_equal, ALU.mult)
                ins.then_inc(pick_w_ready, 1)

            def pair(p, last):
                dve.wait_ge(up_mm, p + 1)
                dve.wait_ge(silu_out, p + 1)
                nc.vector.tensor_tensor(phid, psig, bank[1][:], ALU.mult).then_inc(hid_out, 1)
                if last:
                    nc.vector.sem_inc(moe_ring_free, 1)
                else:
                    take_gathered(p * 2 + 4)
                dve.wait_ge(pick_mm, p + 1)
                nc.vector.tensor_copy(pick_t.rearrange("p t s -> p (t s)"), bank[1][:, 0:TT * P]).then_inc(pick_t_out, 1)
                if not last:
                    make_pick_w(p + 1)
                    make_pick(p + 2)
                dve.wait_ge(down_mm, p * 2 + 2)
                nc.vector.tensor_copy(py[:, 512:1024], bank[3][:]).then_inc(py_out, 1)

            make_pick(0)
            make_pick_w(0)
            take_gathered(2)
            make_pick(1)
            pair(0, False)
            with dve.Fori(1, NPAIR - 1) as p:
                pair(p, False)
            pair(NPAIR - 1, True)
            dve.wait_ge(scat_mm, 1)
            for half in range(2):
                nc.vector.tensor_copy(acc[:, 1, half * 512:(half + 1) * 512], bank[6 + half][:])

        ar.to(m_moe)
        hid = ar.take(2, 4, T)
        sig = ar.take(2, 2, 512)
        dense_filled = [sem(f"dense_filled{i}") for i in range(RING)]
        acc_out = sem("acc_out")
        acc_clear = sem("acc_clear")

        def dense_sync(sp):
            def put(j, src, width):
                sp.dma_start(ring[:, moe_slots[j % RING], :].rearrange("p (k n) -> p k n", n=width), src).then_inc(dense_filled[j % RING], 16)

            put(0, expert_src(wg, 0), 512)
            put(1, expert_src(wu, 0), 512)
            put(2, expert_src(wg, 1), 512)
            sp.wait_ge(gate_mm, 2)
            put(3, expert_src(wd, 0), 1024)
            sp.wait_ge(up_mm, 2)
            put(4, expert_src(wu, 1), 512)
            with sp.Fori(2, NX) as e:
                for j, (w, back, width) in enumerate(((wg, 0, 512), (wd, 1, 1024), (wu, 0, 512))):
                    if j == 0:
                        sp.wait_ge(gate_mm, e * 2)
                    elif j == 1:
                        sp.wait_ge(down_mm, e * 4 - 4)
                    else:
                        sp.wait_ge(up_mm, e * 2)
                    put(2 + j, expert_src(w, e - back if back else e), width)
            sp.wait_ge(gate_mm, 2 * NX)
            put(n_moe - 1, expert_src(wd, NX - 1), 1024)

        def dense_pe(pe):
            def filled(j, n):
                pe.wait_ge(dense_filled[j % RING], n)

            def narrow(slot, b0, signal):
                for f in range(4):
                    for k in range(DT):
                        mm = nc.tensor.matmul(bank[b0 + f // 2][:, (f % 2) * T:(f % 2) * T + T], ring[:, slot, k * 512 + f * P:k * 512 + (f + 1) * P],
                                              H[:, k, 0:T], start=(k == 0), stop=(k == DT - 1), skip_group_check=True)
                    if f % 2:
                        mm.then_inc(signal, 1)

            def down(slot, buf, acc_wait):
                for n in range(4):
                    t, half = n // 2, n % 2
                    acc_wait(n)
                    for f in range(4):
                        mm = nc.tensor.matmul(bank[4 + n][:], hid[:, buf, f, t * P:(t + 1) * P], ring[:, slot, f * 1024 + half * 512:f * 1024 + half * 512 + 512],
                                              start=(f == 0), stop=(f == 3))
                    mm.then_inc(down_mm, 1)

            s = [moe_slots[j % RING] for j in range(RING + 2)]

            def uses(j):
                return 16 * (j // RING + 1)

            filled(0, uses(0))
            narrow(s[0], 0, gate_mm)
            filled(1, uses(1))
            narrow(s[1], 2, up_mm)
            def expert(e, first_time, buf):
                filled(2, e * 16 + (uses(2) - 16))
                pe.wait_ge(silu_out, e * 2)
                narrow(s[2], 0, gate_mm)
                filled(3, e * 16 + (uses(3) - 16))
                pe.wait_ge(hid_out, e * 2)
                down(s[3], 1 - buf, (lambda n: None) if first_time else (lambda n: pe.wait_ge(acc_out, e * 4 + (n + 1 - 8))))
                filled(4, e * 16 + (uses(4) - 16))
                narrow(s[4], 2, up_mm)

            expert(1, True, 1)
            with pe.Fori(2, NX, 2) as e:
                expert(e, False, 0)
                expert(e + 1, False, 1)
            filled(n_moe - 1, uses(n_moe - 1))
            pe.wait_ge(hid_out, 2 * NX)
            down(moe_slots[(n_moe - 1) % RING], (NX - 1) % 2, lambda n: pe.wait_ge(acc_out, 4 * NX + n + 1 - 8))

        def dense_act(act):
            def expert(e, buf, first_time):
                for b in range(2):
                    act.wait_ge(gate_mm, e * 2 + (b + 1))
                    if not first_time:
                        act.wait_ge(hid_out, e * 2 + (b + 1 - 4))
                    nc.scalar.activation(sig[:, buf, b, :], bank[b][:], ACT.Silu).then_inc(silu_out, 1)

            expert(0, 0, True)
            expert(1, 1, True)
            with act.Fori(2, NX, 2) as e:
                expert(e, 0, False)
                expert(e + 1, 1, False)

        def dense_dve(dve):
            def hidden(e, buf):
                for b in range(2):
                    dve.wait_ge(silu_out, e * 2 + (b + 1))
                    dve.wait_ge(up_mm, e * 2 + (b + 1))
                    nc.vector.tensor_tensor(hid[:, buf, :, :].rearrange("p f t -> p (f t)")[:, b * 512:(b + 1) * 512], sig[:, buf, b, :],
                                            bank[2 + b][:], ALU.mult).then_inc(hid_out, 1)

            def gather(e, guard):
                for n in range(4):
                    t, half = n // 2, n % 2
                    dve.wait_ge(down_mm, e * 4 + (n + 1))
                    if guard:
                        dve.wait_ge(acc_out, e * 4 + (n + 1 - 4))
                    a = acc[:, t, half * 512:(half + 1) * 512]
                    col = comb[:, t, bass.ds(e, 1)] if not isinstance(e, int) else comb[:, t, e:e + 1]
                    nc.vector.scalar_tensor_tensor(out=a, in0=bank[4 + n][:], scalar=col, in1=a, op0=ALU.mult, op1=ALU.add).then_inc(acc_out, 1)

            nc.vector.memset(acc, 0.0).then_inc(acc_clear, 1)
            dve.wait_ge(acc_clear, 1)
            hidden(0, 0)
            gather(0, False)
            hidden(1, 1)
            with dve.Fori(1, NX - 1, 2) as e:
                gather(e, True)
                hidden(e + 1, 0)
                gather(e + 1, True)
                hidden(e + 2, 1)
            gather(NX - 1, True)
            nc.vector.sem_inc(moe_ring_free, 1)

        accT_mm, accT_out = sem("accT_mm"), sem("accT_out")
        x_first = sem("x_first")

        def last1_pe(pe):
            for j in range(DT):
                if j >= 4:
                    pe.wait_ge(accT_out, j - 3)
                for t in range(TT):
                    mm = nc.tensor.transpose(bank[j % 4][:, t * P:(t + 1) * P], acc[:, t, j * P:(j + 1) * P], ident[:])
                mm.then_inc(accT_mm, 1)
            norm_pe(pe, H, T)
            norm_pe(pe, H, T2)

        def last1_act(act, chain):
            act.wait_ge(accT_out, DT)
            norm_act(act, X, H, T)
            for k in range(DT):
                act.wait_ge(x_first, k + 1)
                nc.scalar.activation(H[:, k, :], X[:, k, :], ACT.Square).then_inc(sq_ready, 1)
            std_act(act, T2)

        def last1_dve(dve, chain):
            for j in range(DT):
                dve.wait_ge(accT_mm, j + 1)
                nc.vector.scalar_tensor_tensor(out=X[:, j, 0:T], in0=bank[j % 4][:, 0:T], scalar=mod1[:, 40 + j, 0:1],
                                               in1=X[:, j, 0:T], op0=ALU.mult, op1=ALU.add).then_inc(accT_out, 1)
            norm_dve(dve, chain, T)
            for k in range(DT):
                nc.vector.scalar_tensor_tensor(out=X[:, k, 0:T], in0=X[:, k, 0:T], scalar=vec("fng", k, k + 1), in1=rstd[:, 0:T],
                                               op0=ALU.mult, op1=ALU.mult).then_inc(x_first, 1)

        ar.to(0)
        qk = ar.take(16, T2)
        va = ar.take(4, MH, MD + 1)
        yp = ar.take(DT, T2)
        m_mix2 = ar.mark()
        LP, ROWP = 10, 10 + T + PADP
        pp = ar.take(DT, 2, ROWP)
        raw = ar.take(3, 2, T + 2)
        pone, pcum = ar.take(4 * ROWP), ar.take(4 * ROWP)
        pm = ar.take(2, 2, T2)
        pool_w = ar.take(2 * len(POOLS), MD)
        pool_inv = ar.take(len(POOLS), T)
        pool_in, raw_done, pm_done, pool_mm, yp_done, pads_ready = (
            sem("pool_in"), sem("raw_done"), sem("pm_done"), sem("pool_mm"), sem("yp_done"), sem("pads_ready"))
        P9 = 48
        NPOOL = len(POOLS)

        def in2_pe(pe):
            def gates(k):
                mm = nc.tensor.matmul(bank[6][:], gate_w[:, k, :], H[:, k, :], start=(k == 0), stop=(k == DT - 1))
                if k == DT - 1:
                    mm.then_inc(gates_mm, 1)

            proj_first(pe, AT_SECOND, h_all, T2, lambda k: 3 * DT + 2 * k + 2, gates)
            for n in range(1, 10):
                c = AT_SECOND + n
                chunk_wait(pe, c)
                for j in range(4):
                    if n in (4, 5):
                        proj_rows(pe, c, j, j == 3)
                    else:
                        proj_tile(pe, c, j, h_all, T2, j == 3)
                if n == 1:
                    mgate_pe(pe)
            for g in range(NPOOL):
                pe.wait_ge(pool_in, 32)
                pe.wait_ge(pm_done, g + 1)
                for j in range(2):
                    n = 2 * g + j
                    if n >= 2:
                        pe.wait_ge(yp_done, n - 1)
                    for k in range(2):
                        mm = nc.tensor.matmul(bank[4 + n % 2][:], pool_w[:, 2 * g + k, j * P:(j + 1) * P], pm[:, g % 2, k, :],
                                              start=(k == 0), stop=(k == 1))
                    mm.then_inc(pool_mm, 1)

        def in2_act(act, chain):
            act.dma_start(pool_w, d["ab_pool_w_2"].rearrange("g (k p) n -> p (g k) n", p=P)).then_inc(pool_in, 16)
            act.dma_start(pool_inv, d["pool_inv"]).then_inc(pool_in, 16)
            act.dma_start(m_mask, d["m_mask"]).then_inc(mmask_in, 16)
            modulate_act(act, mod2, 0, True)
            mgate_act(act, chain)
            act.wait_ge(pads_ready, 1)
            for n in range(16):
                if n == 3:
                    mgate_exp_act(act)
                b = next_tile(act)[:].rearrange("p (s t) -> p s t", s=2)
                if n >= 3:
                    act.wait_ge(raw_done, n - 2)
                nc.scalar.copy(raw[:, n % 3, :, 1:T + 1], b).then_inc(proj_out, 1)
            for c in range(2):
                for t in range(4):
                    b = next_tile(act)[:].rearrange("p (h e) -> p h e", h=2)
                    nc.scalar.copy(va[:, t, 2 * c:2 * c + 2, 0:MD], b).then_inc(proj_out, 1)
            for n in range(DT):
                b = next_tile(act)[:].rearrange("p (s t) -> p s t", s=2)
                nc.scalar.copy(pp[:, n, :, LP:LP + T], b).then_inc(proj_out, 1)
            for n in range(DT):
                b = next_tile(act)
                nc.scalar.activation(yp[:, n, :], b[:], ACT.Silu).then_inc(proj_out, 1)

        def in2_dve(dve, chain):
            norm_dve(dve, chain, T2)
            coef_dve(chain, vec("gpre", 0, 8), mod2, 8, True)
            modulate_dve(dve, True)
            nc.vector.memset(raw, 0.0)
            nc.vector.memset(va[:, :, :, MD:MD + 1], 1.0)
            nc.vector.memset(pone, 1.0)
            ck = vec("acv").rearrange("p (w n) -> p w n", w=3)[:, :, 8:16]
            nc.vector.tensor_scalar(ck, ck, MD ** -0.5, None, ALU.mult)
            nc.vector.memset(pp, 0.0).then_inc(pads_ready, 1)
            mgate_dve(dve, chain)
            for n in range(16):
                if n == 6:
                    mgate_cols_dve(dve, chain)
                dve.wait_ge(proj_out, P9 + n + 1)
                u = qk[:, n, :].rearrange("p (s t) -> p s t", s=2)
                chain.link(nc.vector.tensor_scalar(u, raw[:, n % 3, :, 0:T], vec("acv", n, n + 1), None, ALU.mult))
                chain.link(nc.vector.scalar_tensor_tensor(out=u, in0=raw[:, n % 3, :, 1:T + 1], scalar=vec("acv", 16 + n, 17 + n), in1=u, op0=ALU.mult, op1=ALU.add))
                nc.vector.scalar_tensor_tensor(out=u, in0=raw[:, n % 3, :, 2:T + 2], scalar=vec("acv", 32 + n, 33 + n), in1=u, op0=ALU.mult, op1=ALU.add).then_inc(raw_done, 1)
            dve.wait_ge(pool_in, 32)
            for g in range(NPOOL + 1):
                if g < NPOOL:
                    half = POOLS[g] // 2
                    dve.wait_ge(proj_out, P9 + 24 + 2 * g + 2)
                    row = pp[:, 2 * g:2 * g + 2, :, :].rearrange("p k s t -> p (k s t)")
                    chain.link(nc.vector.tensor_tensor_scan(pcum, pone, row, 0.0, ALU.mult, ALU.add))
                    cu = pcum.rearrange("p (r t) -> p r t", t=ROWP)
                    o = pm[:, g % 2, :, :].rearrange("p k (s t) -> p (k s) t", s=2)
                    if g >= 2:
                        dve.wait_ge(pool_mm, 2 * g - 2)
                    chain.link(nc.vector.tensor_tensor(o, cu[:, :, LP + half - 1:LP + half - 1 + T], cu[:, :, LP - half - 1:LP - half - 1 + T], ALU.subtract))
                    chain.link(nc.vector.tensor_tensor(o, o, bc(pool_inv[:, g, :].unsqueeze(1), [P, 4, T]), ALU.mult))
                    nc.vector.tensor_tensor(o, o, pp[:, 2 * g:2 * g + 2, :, LP:LP + T].rearrange("p k s t -> p (k s) t"), ALU.subtract).then_inc(pm_done, 1)
                if g >= 1:
                    dve.wait_ge(proj_out, P9 + 40)
                    for n in (2 * g - 2, 2 * g - 1):
                        dve.wait_ge(pool_mm, n + 1)
                        nc.vector.scalar_tensor_tensor(out=yp[:, n, :], in0=bank[4 + n % 2][:], scalar=vec("psc", n, n + 1), in1=yp[:, n, :],
                                                       op0=ALU.mult, op1=ALU.mult).then_inc(yp_done, 1)

        gmask = ar.take(T2)
        mprev, mlast, mdec = ar.take(4), ar.take(4), ar.take(4)
        gr, ge1, lf, ga_, gm_, gw1, gw2, gw3 = (yp[:, n, :] for n in range(DT))
        negM = rstd[:]
        m_mask = csil[:].rearrange("p b k n -> p (b k n)")[:, 0:2 * P].rearrange("p (d t) -> p d t", d=2)
        ORDER = ((2, 3, 0, 1), (3, 2, 1, 0))
        gr_ready, g_neg, g_exp, w_arg, w_exp, gT_mm, mmask_in, gates_mm = (sem("gr_ready"), sem("g_neg"), sem("g_exp"), sem("w_arg"), sem("w_exp"), sem("gT_mm"), sem("mmask_in"), sem("gates_mm"))

        def mgate_pe(pe):
            pe.wait_ge(w_exp, 1)
            for q, src in enumerate((ga_, gw1, gw2, gw3)):
                for c in range(4):
                    mm = nc.tensor.transpose(bank[4 + q // 2][:, ((q % 2) * 4 + c) * 64:((q % 2) * 4 + c + 1) * 64], src[0:64, c * P:(c + 1) * P], ident[0:64, 0:64])
            mm.then_inc(gT_mm, 1)
            for dr in range(2):
                for h in range(MH):
                    r = 32 * dr + h
                    mm = nc.tensor.matmul(bank[7][:, (dr * MH + h) * 4:(dr * MH + h) * 4 + 4], bc(ident[0:64, r:r + 1], [64, P]), mdec[0:64, :],
                                          start=True, stop=True, skip_group_check=True)
            mm.then_inc(gT_mm, 1)

        def mgate_act(act, chain):
            act.wait_ge(gates_mm, 1)
            nc.scalar.activation(gr, bank[6][:], ACT.Identity, bias=vec("gb")).then_inc(gr_ready, 1)
            act.wait_ge(g_neg, 1)
            chain.link(nc.scalar.activation(ge1, ge1, ACT.Exp))
            nc.scalar.activation(ge1, ge1, ACT.Ln, bias=ones[:, 0:1]).then_inc(g_exp, 1)

        def mgate_exp_act(act):
            act.wait_ge(w_arg, 1)
            for w in (gw1, gw2, gw3):
                nc.scalar.activation(w[0:64, :], w[0:64, :], ACT.Exp)
            nc.scalar.activation(mdec[0:64, :], mdec[0:64, :], ACT.Exp).then_inc(w_exp, 1)

        def mgate_dve(dve, chain):
            L, V = chain.link, nc.vector
            R = slice(0, 64)
            L(V.memset(gmask, 1.0))
            L(V.memset(gmask.rearrange("p (c t) -> p c t", t=P)[:, :, 0:1], 0.0))
            L(V.memset(mprev, 0.0))
            dve.wait_ge(gr_ready, 1)
            V.scalar_tensor_tensor(out=ge1, in0=gr, scalar=-1.0, in1=gr, op0=ALU.mult, op1=ALU.min).then_inc(g_neg, 1)
            dve.wait_ge(g_exp, 1)
            L(V.scalar_tensor_tensor(out=ge1, in0=gr, scalar=0.0, in1=ge1, op0=ALU.min, op1=ALU.subtract))
            L(V.tensor_copy(gw1[R, :], ge1[64:128, :]))
            b = lf
            L(V.tensor_tensor_scan(b[0:32, :], gmask[0:32, :], gw1[0:32, :], 0.0, ALU.mult, ALU.add))
            L(V.tensor_tensor_scan(b[32:64, ::-1], gmask[32:64, :], gw1[32:64, ::-1], 0.0, ALU.mult, ALU.add))
            L(V.tensor_tensor(ga_[R, :], gr[R, :], b[R, :], ALU.subtract))
            for step in range(4):
                for dr in range(2):
                    rows = slice(32 * dr, 32 * dr + 32)
                    c = ORDER[dr][step]
                    s = slice(c * P, (c + 1) * P)
                    back = 1 if dr == 0 else -1
                    end = P - 1 if dr == 0 else 0
                    x = ga_[rows, s][:, ::back]
                    L(V.tensor_tensor_scan(gm_[rows, s][:, ::back], x, x, mprev[rows, c:c + 1], ALU.max, ALU.max))
                    L(V.tensor_copy(mlast[rows, c:c + 1], gm_[rows, c * P + end:c * P + end + 1]))
                    if step < 3:
                        nx = ORDER[dr][step + 1]
                        L(V.tensor_tensor(mprev[rows, nx:nx + 1], mlast[rows, c:c + 1], b[rows, c * P + end:c * P + end + 1], ALU.add))

            def ch(x):
                return x[R, :].rearrange("p (c t) -> p c t", t=P)

            shape = [64, 4, P]
            L(V.tensor_tensor(ch(gw1), bc(mprev[R, :].unsqueeze(2), shape), ch(gm_), ALU.subtract))
            L(V.scalar_tensor_tensor(out=gw2[R, :], in0=b[R, :], scalar=-1.0, in1=gm_[R, :], op0=ALU.mult, op1=ALU.subtract))
            L(V.tensor_tensor(ch(gw3), ch(ga_), bc(mlast[R, :].unsqueeze(2), shape), ALU.subtract))
            L(V.tensor_scalar(negM[R, :], gm_[R, :], -1.0, None, ALU.mult))
            V.tensor_tensor(mdec[R, :], mprev[R, :], mlast[R, :], ALU.subtract).then_inc(w_arg, 1)

        def mgate_cols_dve(dve, chain):
            L, V = chain.link, nc.vector
            dve.wait_ge(gT_mm, 1)
            for q in range(4):
                v = bank[4 + q // 2][:, (q % 2) * 256:(q % 2) * 256 + 256].rearrange("p (c d h) -> p c d h", c=4, d=2)
                L(V.tensor_copy(mcols[:, q, :, :, :], v[:, :, :, 0:MH]))
            dve.wait_ge(gT_mm, 2)
            L(V.tensor_copy(decay_b[:].rearrange("p d h c -> p (d h c)"), bank[7][:, 0:32]))
            dve.wait_ge(mmask_in, 16)

        ar.to(m_mix2)
        hn = ar.take(4, MH, MD)
        hT = ar.take(DT, T2)
        xe = ar.take(2, T2)
        kw = ar.take(2, 4, MD)
        cst = ar.take(2, 2, MD + 1)
        t1 = ar.take(2, MD + 1)
        t2 = ar.take(2, MD + 1)
        dn = ar.take(2, 1)
        (rs_mm, kT_mm, mb_mm, xa_done, xe_done, s_done, kw_done, intra_mm, cross_mm, upd_mm, t1_done, t2_done, cst_done, hn_done, hT_mm, hT_out) = (
            sem(n) for n in ("rs_mm", "kT_mm", "mb_mm", "xa_done", "xe_done", "s_done", "kw_done", "intra_mm", "cross_mm", "upd_mm",
                             "t1_done", "t2_done", "cst_done", "hn_done", "hT_mm", "hT_out"))

        def mlstm_pe(pe):
            def prepare(h):
                if h:
                    pe.wait_ge(cst_done, 12 * h)
                for dr in range(2):
                    r = 32 * dr + h
                    nc.tensor.matmul(bank[2 + dr][:], bc(ident[0:64, r:r + 1], [64, P]), negM[0:64, :], start=True, stop=True).then_inc(mb_mm, 1)
                for c in range(4):
                    for j in range(2):
                        mm = nc.tensor.transpose(bank[6 + c // 2][:, ((c % 2) * 2 + j) * P:((c % 2) * 2 + j + 1) * P],
                                                 qk[:, 8 + 2 * h + j, c * P:(c + 1) * P], ident[:])
                    if c % 2:
                        mm.then_inc(kT_mm, 1)
                if h:
                    pe.wait_ge(t1_done, 6 * h)
                for c in range(4):
                    s = slice(c * P, (c + 1) * P)
                    for j in range(2):
                        mm = nc.tensor.matmul(bank[5][:, s], qk[:, 8 + 2 * h + j, s], qk[:, 2 * h + j, s], start=(j == 0), stop=(j == 1), skip_group_check=True)
                mm.then_inc(rs_mm, 1)

            prepare(0)
            for h in range(MH):
                pe.wait_ge(kw_done, 8 * (h + 1))
                if h:
                    pe.wait_ge(t2_done, 8 * h)
                    pe.wait_ge(hT_out, 2 * h)
                for step in range(4):
                    for dr in range(2):
                        c = ORDER[dr][step]
                        s = slice(c * P, (c + 1) * P)
                        n = 4 * h + step
                        if step == 0 and dr == 0:
                            pe.wait_ge(s_done, 2 * h + 2)
                        if step:
                            pe.wait_ge(t2_done, 2 * (n - 1) + dr + 1)
                        nc.tensor.matmul(bank[4 * dr][:, 0:MD + 1], xe[:, dr, s], va[:, c, h, :], start=True, stop=True).then_inc(intra_mm, 1)
                        if step < 3:
                            if step:
                                pe.wait_ge(cst_done, 12 * h + 4 * (step - 1) + 2 * dr + 2)
                            for j in range(2):
                                nc.tensor.matmul(bank[4 * dr + 2 + j][:, 0:MD + 1], kw[:, dr, c, j * P:(j + 1) * P], va[:, c, h, :],
                                                 start=True, stop=True).then_inc(upd_mm, 1)
                        if step:
                            pe.wait_ge(cst_done, 12 * h + 4 * (step - 1) + 2 * dr + 2)
                            for j in range(2):
                                mm = nc.tensor.matmul(bank[4 * dr + 1][:, 0:MD + 1], qk[:, 2 * h + j, s], cst[:, dr, j, :], start=(j == 0), stop=(j == 1))
                            mm.then_inc(cross_mm, 1)
                if h < MH - 1:
                    prepare(h + 1)
                pe.wait_ge(hn_done, 8 * (h + 1))
                for j in range(2):
                    for c in range(4):
                        mm = nc.tensor.transpose(bank[1 - j][:, c * P:(c + 1) * P], hn[:, c, h, j * P:(j + 1) * P], ident[:])
                    mm.then_inc(hT_mm, 1)

        def mlstm_act(act, chain):
            def prepare(h):
                for dr in range(2):
                    act.wait_ge(xa_done, 2 * h + dr + 1)
                    for c in range(4):
                        s = slice(c * P, (c + 1) * P)
                        ins = nc.scalar.activation(xe[:, dr, s], xe[:, dr, s], ACT.Exp, bias=mcols[:, 0, c, dr, h:h + 1])
                    ins.then_inc(xe_done, 1)
                for c in range(4):
                    act.wait_ge(kT_mm, 2 * h + c // 2 + 1)
                    for dr in range(2):
                        nc.scalar.activation(kw[:, dr, c, :], bank[6 + c // 2][:, (c % 2) * MD:(c % 2) * MD + MD], ACT.Copy,
                                             scale=mcols[:, 3, c, dr, h:h + 1]).then_inc(kw_done, 1)

            prepare(0)
            for h in range(MH):
                for step in range(1, 4):
                    for dr in range(2):
                        c = ORDER[dr][step]
                        n = 3 * h + step - 1
                        act.wait_ge(cross_mm, 2 * n + dr + 1)
                        act.wait_ge(t2_done, 2 * (4 * h + step - 1) + dr + 1)
                        nc.scalar.activation(t1[:, dr, :], bank[4 * dr + 1][:, 0:MD + 1], ACT.Copy, scale=mcols[:, 1, c, dr, h:h + 1]).then_inc(t1_done, 1)
                if h < MH - 1:
                    prepare(h + 1)
                for j in range(2):
                    act.wait_ge(hT_mm, 2 * h + j + 1)
                    nc.scalar.copy(hT[:, 2 * h + j, :], bank[1 - j][:]).then_inc(hT_out, 1)

        def mlstm_dve(dve, chain):
            L, V = chain.link, nc.vector
            for h in range(MH):
                for dr in range(2):
                    dve.wait_ge(mb_mm, 2 * h + dr + 1)
                    if h:
                        dve.wait_ge(intra_mm, 8 * h)
                    V.tensor_tensor(xe[:, dr, :].rearrange("p (c t) -> p c t", t=P), bank[2 + dr][:].rearrange("p (c t) -> p c t", t=P),
                                    bc(m_mask[:, dr, :].unsqueeze(1), [P, 4, P]), ALU.add).then_inc(xa_done, 1)
                dve.wait_ge(rs_mm, h + 1)
                for dr in range(2):
                    dve.wait_ge(xe_done, 2 * h + dr + 1)
                    V.tensor_tensor(xe[:, dr, :], xe[:, dr, :], bank[5][:], ALU.mult).then_inc(s_done, 1)
                seen = set()
                for step in range(4):
                    for dr in range(2):
                        c = ORDER[dr][step]
                        dve.wait_ge(intra_mm, 8 * h + 2 * step + dr + 1)
                        o = bank[4 * dr][:, 0:MD + 1]
                        if step:
                            dve.wait_ge(t1_done, 6 * h + 2 * (step - 1) + dr + 1)
                            V.tensor_tensor(t2[:, dr, :], t1[:, dr, :], o, ALU.add).then_inc(t2_done, 1)
                        else:
                            V.tensor_copy(t2[:, dr, :], o).then_inc(t2_done, 1)
                        dve.wait_ge(t2_done, 2 * (4 * h + step) + dr + 1)
                        x = t2[:, dr, MD:MD + 1]
                        L(V.scalar_tensor_tensor(out=dn[:, dr, :], in0=x, scalar=-1.0, in1=x, op0=ALU.mult, op1=ALU.max))
                        L(V.tensor_tensor(dn[:, dr, :], dn[:, dr, :], mcols[:, 2, c, dr, h:h + 1], ALU.max))
                        L(V.reciprocal(dn[:, dr, :], dn[:, dr, :]))
                        if c in seen:
                            V.scalar_tensor_tensor(out=hn[:, c, h, :], in0=t2[:, dr, 0:MD], scalar=dn[:, dr, :], in1=hn[:, c, h, :], op0=ALU.mult, op1=ALU.add).then_inc(hn_done, 1)
                        else:
                            V.tensor_scalar(hn[:, c, h, :], t2[:, dr, 0:MD], dn[:, dr, :], None, ALU.mult).then_inc(hn_done, 1)
                        seen.add(c)
                        if step < 3:
                            if step:
                                dve.wait_ge(cross_mm, 6 * h + 2 * (step - 1) + dr + 1)
                            for j in range(2):
                                dve.wait_ge(upd_mm, 12 * h + 4 * step + 2 * dr + j + 1)
                                o = bank[4 * dr + 2 + j][:, 0:MD + 1]
                                if step:
                                    V.scalar_tensor_tensor(out=cst[:, dr, j, :], in0=cst[:, dr, j, :], scalar=decay_b[:, dr, h, c:c + 1], in1=o,
                                                           op0=ALU.mult, op1=ALU.add).then_inc(cst_done, 1)
                                else:
                                    V.tensor_copy(cst[:, dr, j, :], o).then_inc(cst_done, 1)

        ar.to(0)
        so = ar.take(DT, T2)
        sz = ar.take(DT, T2)
        hr = ar.take(MH, T2)
        assert ar.at <= 8192 + 4112
        o_mul, o_sq, hs_mm, hs_std, ym_done = (sem("o_mul"), sem("o_sq"), sem("hs_mm"), sem("hs_std"), sem("ym_done"))
        yo = so
        P12 = P9 + 40

        def slot_q(c, k, a, b):
            return ring[:, chunks[c][1], k * 256 + a:k * 256 + b]

        def out2_pe(pe):
            for n in range(10, 14):
                c = AT_SECOND + n
                chunk_wait(pe, c)
                for j in range(4):
                    proj_tile(pe, c, j, h_all, T2, j == 3)
            def pooled_half(j):
                c = AT_SECOND + 14 + j // 2
                chunk_wait(pe, c)
                pe.wait_ge(proj_out, projected[0] + j - NB + 1)
                for k in range(8, 16):
                    nc.tensor.matmul(bank[(projected[0] + j) % NB][:], slot_q(c, k, (j % 2) * P, (j % 2 + 1) * P), yp[:, k - 8, :], start=(k == 8), stop=False)

            def mlstm_half(j):
                c = AT_SECOND + 14 + j // 2
                for k in range(8):
                    mm = nc.tensor.matmul(bank[(projected[0] + j) % NB][:], slot_q(c, k, (j % 2) * P, (j % 2 + 1) * P), hT[:, k, :], start=False, stop=(k == 7))
                mm.then_inc(proj_mm, 1)
                last_use[c] = (proj_mm, projected[0] + j + 1)

            for j in range(2):
                pooled_half(j)
            for h in range(MH):
                pe.wait_ge(o_sq, 2 * h + 2)
                for j in range(2):
                    mm = nc.tensor.matmul(bank[4 + h][:], ones[:], so[:, 2 * h + j, :], start=(j == 0), stop=(j == 1))
                mm.then_inc(hs_mm, 1)
            for j in range(2, 4):
                pooled_half(j)
            pe.wait_ge(ym_done, DT)
            for j in range(4):
                mlstm_half(j)
            for j in range(4, DT):
                pooled_half(j)
                mlstm_half(j)
            projected[0] += DT
            norm_pe(pe, H, T2)
            norm_pe(pe, H, T2)

        def out2_act(act, chain):
            for n in range(DT):
                b = next_tile(act)
                nc.scalar.activation(so[:, n, :], b[:], ACT.Sigmoid).then_inc(proj_out, 1)
            for n in range(DT):
                b = next_tile(act)
                nc.scalar.activation(sz[:, n, :], b[:], ACT.Silu).then_inc(proj_out, 1)
                act.wait_ge(o_mul, n + 1)
                nc.scalar.activation(so[:, n, :], hT[:, n, :], ACT.Square).then_inc(o_sq, 1)
            for h in range(MH):
                act.wait_ge(hs_mm, h + 1)
                nc.scalar.activation(hr[:, h, :], bank[4 + h][:], ACT.Sqrt, bias=epsc[:], scale=1.0 / MD).then_inc(hs_std, 1)
            for n in range(DT):
                b = next_tile(act)
                nc.scalar.copy(yo[:, n, :], b[:]).then_inc(proj_out, 1)
            act.wait_ge(proj_out, P12 + 24)
            norm_act(act, yo, H, T2)
            for k in range(DT):
                act.wait_ge(x_new, k + 1)
                nc.scalar.activation(H[:, k, :], X[:, k, :], ACT.Square).then_inc(sq_ready, 1)
            std_act(act, T2)

        x_new = sem("x_new")

        def post_dve(dve, chain, layer, both):
            L, V = chain.link, nc.vector
            n = T2 if both else T
            for j in range(1 + both):
                L(V.tensor_tensor(gcoef[:, j, :], vec("gpost", 8 * layer, 8 * layer + 8), mod2[:, 24 * layer + 16:24 * layer + 24, j], ALU.mult))
            norm_dve(dve, chain, n)
            scaled_to = {}
            for k in range(DT + 1):
                if k < DT:
                    for j in range(1 + both):
                        s = slice(j * T, (j + 1) * T)
                        V.scalar_tensor_tensor(out=yo[:, k, s], in0=yo[:, k, s], scalar=gcoef[:, j, k:k + 1], in1=rstd[:, s],
                                               op0=ALU.mult, op1=ALU.mult).then_inc(chain.s, 1)
                        chain.n += 1
                    scaled_to[k] = chain.n
                if k >= 1:
                    dve.wait_ge(chain.s, scaled_to[k - 1])
                    V.tensor_tensor(X[:, k - 1, 0:n], X[:, k - 1, 0:n], yo[:, k - 1, 0:n], ALU.add).then_inc(x_new, 1)

        def out2_dve(dve, chain):
            L, V = chain.link, nc.vector
            for n in range(DT):
                dve.wait_ge(proj_out, P12 + n + 1)
                V.tensor_tensor(hT[:, n, :], hT[:, n, :], so[:, n, :], ALU.mult).then_inc(o_mul, 1)
            for h in range(MH):
                dve.wait_ge(hs_std, h + 1)
                L(V.reciprocal(hr[:, h, :], hr[:, h, :]))
                for j in range(2):
                    n = 2 * h + j
                    L(V.scalar_tensor_tensor(out=hT[:, n, :], in0=hT[:, n, :], scalar=vec("mng", n, n + 1), in1=hr[:, h, :], op0=ALU.mult, op1=ALU.mult))
                    dve.wait_ge(proj_out, P12 + 8 + n + 1)
                    V.tensor_tensor(hT[:, n, :], hT[:, n, :], sz[:, n, :], ALU.mult).then_inc(ym_done, 1)
            post_dve(dve, chain, 0, True)

        ar.to(0)
        yo_keep = ar.take(DT, T2)
        aq = ar.take(DT, T)
        ak = ar.take(2, T2)
        av = ar.take(4, AKV * AD)
        az = ar.take(DT, T)
        aqz = ar.take(2 * DT, T)
        m_att = ar.mark()
        rope = ar.take(2, T)
        swap = ar.take(P)
        rt = ar.take(2, T)
        rope_in, swap_mm, rope_done, amask_in = sem("rope_in"), sem("swap_mm"), sem("rope_done"), sem("amask_in")
        P13 = P12 + 24

        def in3_pe(pe):
            proj_first(pe, AT_C, h_x, T, lambda k: 5 * DT + 2 * k + 2)
            for n in range(1, 5):
                c = AT_C + n
                chunk_wait(pe, c)
                if n == 2:
                    for j in range(2):
                        proj_tile(pe, c, j, h_all, T2, False)
                    for t in range(4):
                        i = projected[0]
                        projected[0] += 1
                        pe.wait_ge(proj_out, i - NB + 1)
                        for k in range(DT):
                            mm = nc.tensor.matmul(bank[i % NB][:, 0:256], H[:, k, t * P:(t + 1) * P], slot_k(c, k, 256, 512), start=(k == 0), stop=(k == DT - 1))
                        mm.then_inc(proj_mm, 1)
                        last_use[c] = (proj_mm, i + 1)
                else:
                    for j in range(4):
                        proj_tile(pe, c, j, h_x, T, j == 3)
            pe.wait_ge(rope_in, 32)
            for n in range(10):
                src = aq[:, n, :] if n < 8 else ak[:, n - 8, 0:T]
                if n == 0:
                    pe.wait_ge(proj_out, P13 + 22)
                if n >= 2:
                    pe.wait_ge(rope_done, n - 1)
                nc.tensor.matmul(bank[4 + n % 2][:, 0:T], swap, src, start=True, stop=True).then_inc(swap_mm, 1)

        def in3_act(act, chain):
            act.dma_start(rope, d["rope"]).then_inc(rope_in, 16)
            act.dma_start(swap, d["swap"]).then_inc(rope_in, 16)
            modulate_act(act, mod2, 24, True)
            for n in range(8):
                b = next_tile(act)
                nc.scalar.activation(aq[:, n, :], b[:, 0:T], ACT.Copy, scale=AD ** -0.5).then_inc(proj_out, 1)
            for n in range(2):
                b = next_tile(act)
                nc.scalar.copy(ak[:, n, :], b[:]).then_inc(proj_out, 1)
            for t in range(4):
                b = next_tile(act)
                nc.scalar.copy(av[:, t, :], b[:, 0:256]).then_inc(proj_out, 1)
            for n in range(8):
                b = next_tile(act)
                nc.scalar.activation(az[:, n, :], b[:, 0:T], ACT.Silu).then_inc(proj_out, 1)

        def in3_dve(dve, chain):
            L, V = chain.link, nc.vector
            norm_dve(dve, chain, T2)
            coef_dve(chain, vec("gpre", 8, 16), mod2, 32, True)
            modulate_dve(dve, True)
            L(V.memset(aqz, 0.0))
            dve.wait_ge(rope_in, 32)
            for n in range(10):
                x = aq[:, n, :] if n < 8 else ak[:, n - 8, 0:T]
                dve.wait_ge(swap_mm, n + 1)
                V.tensor_tensor(rt[:, 0, :], x, rope[:, 0, :], ALU.mult)
                L(V.tensor_tensor(rt[:, 1, :], bank[4 + n % 2][:, 0:T], rope[:, 1, :], ALU.mult))
                if n < 8:
                    V.tensor_tensor(aqz[0:AD, 2 * n, :], rt[0:AD, 0, :], rt[0:AD, 1, :], ALU.add)
                    V.tensor_tensor(aqz[AD:P, 2 * n + 1, :], rt[AD:P, 0, :], rt[AD:P, 1, :], ALU.add).then_inc(rope_done, 1)
                else:
                    V.tensor_tensor(x, rt[:, 0, :], rt[:, 1, :], ALU.add).then_inc(rope_done, 1)
                dve.wait_ge(rope_done, n + 1)

        ar.to(m_att)
        NU = DT * 2 * TT
        am = ar.take(TT, P)
        NPB = 4
        pr = ar.take(NPB, T2)
        pT = ar.take(2, 4, P)
        amx, asum, asink, arec = ar.take(NU), ar.take(NU), ar.take(NU), ar.take(NU)
        as_mm, amax_done, p_exp, p_done, pT_mm, pT_out, pv_mm, oz_done = (sem(n) for n in ("as_mm", "amax_done", "p_exp", "p_done", "pT_mm", "pT_out", "pv_mm", "oz_done"))

        def unit(u):
            i, a, t = u // 4, (u // 2) % 2, u % 2
            m, g = divmod(i, 4)
            return i, a, t, m, 8 * m + 4 * a + g

        def att_pe(pe):
            for u in range(NU + 3):
                if u < NU:
                    i, a, t, m, head = unit(u)
                    if u == 0:
                        pe.wait_ge(amask_in, 32)
                    if u >= 3:
                        pe.wait_ge(p_exp, u - 2)
                    b = bank[u % 3]
                    nc.tensor.matmul(b[:], aqz[:, 2 * i + a, t * P:(t + 1) * P], ak[:, m, :], start=True, stop=False, skip_group_check=True)
                    o = (1 - t) * P
                    nc.tensor.matmul(b[:, o:o + P], ident[:], am[:, t, :], start=False, stop=True, skip_group_check=True).then_inc(as_mm, 1)
                if 0 <= u - 2 < NU:
                    v = u - 2
                    pe.wait_ge(p_done, v + 1)
                    if v >= 2:
                        pe.wait_ge(pT_out, v - 1)
                    for s in range(4):
                        mm = nc.tensor.transpose(bank[3 + v % 2][:, s * P:(s + 1) * P], pr[:, v % NPB, s * P:(s + 1) * P], ident[:])
                    mm.then_inc(pT_mm, 1)
                if u - 3 >= 0:
                    v = u - 3
                    i, a, t, m, head = unit(v)
                    kv = 2 * m + a
                    pe.wait_ge(pT_out, v + 1)
                    if v % 4 == 0 and i >= 2:
                        pe.wait_ge(oz_done, i - 1)
                    for s in range(4):
                        mm = nc.tensor.matmul(bank[5 + i % 2][AD * a:AD * a + AD, t * P:(t + 1) * P], av[:, s, kv * AD:(kv + 1) * AD], pT[:, v % 2, s, :],
                                              start=(s == 0), stop=(s == 3), skip_group_check=True)
                    mm.then_inc(pv_mm, 1)

        def att_act(act, chain):
            act.dma_start(am[:, 0, :], d["a_mask"][:, 0, P:T]).then_inc(amask_in, 16)
            act.dma_start(am[:, 1, :], d["a_mask"][:, 1, 0:P]).then_inc(amask_in, 16)
            for u in range(NU + 2):
                if u < NU:
                    i, a, t, m, head = unit(u)
                    act.wait_ge(amax_done, u + 1)
                    if u >= NPB:
                        act.wait_ge(pT_mm, u - NPB + 1)
                    nc.scalar.activation(asink[:, u:u + 1], sink_b[:, head:head + 1], ACT.Exp, bias=amx[:, u:u + 1])
                    nc.scalar.activation(pr[:, u % NPB, :], bank[u % 3][:], ACT.Exp, bias=amx[:, u:u + 1], accum_out=asum[:, u:u + 1]).then_inc(p_exp, 1)
                if u >= 2:
                    v = u - 2
                    act.wait_ge(pT_mm, v + 1)
                    if v >= 2:
                        act.wait_ge(pv_mm, v - 1)
                    nc.scalar.copy(pT[:, v % 2, :, :].rearrange("p s t -> p (s t)"), bank[3 + v % 2][:]).then_inc(pT_out, 1)

        def att_dve(dve, chain):
            L, V = chain.link, nc.vector
            for u in range(NU + 1):
                if u < NU:
                    i, a, t, m, head = unit(u)
                    dve.wait_ge(as_mm, u + 1)
                    L(V.tensor_reduce(amx[:, u:u + 1], bank[u % 3][:], AXX, ALU.max))
                    V.tensor_scalar(amx[:, u:u + 1], amx[:, u:u + 1], sink_b[:, head:head + 1], -1.0, ALU.max, ALU.mult).then_inc(amax_done, 1)
                if u >= 1:
                    v = u - 1
                    dve.wait_ge(p_exp, v + 1)
                    L(V.tensor_tensor(arec[:, v:v + 1], asum[:, v:v + 1], asink[:, v:v + 1], ALU.add))
                    L(V.reciprocal(arec[:, v:v + 1], arec[:, v:v + 1]))
                    V.tensor_scalar(pr[:, v % NPB, :], pr[:, v % NPB, :], arec[:, v:v + 1], None, ALU.mult).then_inc(p_done, 1)
                if u % 4 == 1 and u >= 9 or u == NU:
                    for i in ([u // 4 - 2] if u < NU else [u // 4 - 2, u // 4 - 1]):
                        dve.wait_ge(pv_mm, 4 * i + 4)
                        V.tensor_tensor(az[:, i, :], az[:, i, :], bank[5 + i % 2][:, 0:T], ALU.mult).then_inc(oz_done, 1)

        def out3_pe(pe):
            for n in range(2):
                c = AT_CO + n
                chunk_wait(pe, c)
                for j in range(4):
                    proj_tile(pe, c, j, lambda k: az[:, k, :], T, j == 3)
            norm_pe(pe, H, T)

        def out3_act(act, chain):
            for n in range(DT):
                b = next_tile(act)
                nc.scalar.copy(yo[:, n, 0:T], b[:, 0:T]).then_inc(proj_out, 1)
            act.wait_ge(proj_out, P13 + 22 + 8)
            norm_act(act, yo, H, T)

        def out3_dve(dve, chain):
            post_dve(dve, chain, 1, False)

        RUN = [(mod_pe, mod_act, mod_dve), (in1_pe, in1_act, in1_dve), (gla_pe, gla_act, gla_dve), (hy_pe, hy_act, hy_dve),
               (merge_pe, merge_act, merge_dve), (router_pe, router_act, router_dve), (moe_pe, moe_act, moe_dve),
               (last1_pe, last1_act, last1_dve), (in2_pe, in2_act, in2_dve), (mlstm_pe, mlstm_act, mlstm_dve),
               (out2_pe, out2_act, out2_dve), (in3_pe, in3_act, in3_dve), (att_pe, att_act, att_dve), (out3_pe, out3_act, out3_dve)]
        N_STAGES = len(RUN)

        block = ctx.enter_context(nc.Block())

        @block.scalar
        def _(act):
            chain = Chain(act, act_step)
            loads_act(act)
            for n, (_, f, _) in enumerate(RUN):
                if f is not None:
                    f(act, chain)
                stage_end(act, "act")

        @block.vector
        def _(dve):
            chain = Chain(dve, dve_step)
            for n, (_, _, f) in enumerate(RUN):
                if f is not None:
                    f(dve, chain)
                stage_end(dve, "dve")

        @block.tensor
        def _(pe):
            for n, (f, _, _) in enumerate(RUN):
                if f is not None:
                    f(pe)
                stage_end(pe, "pe")

        @block.sync
        def _(sp):
            loads_sync(sp)
            for c in range(N_FIRST):
                loads_rest_sync(sp, c)
                load_chunk(sp, c)
            moe_sync(sp)
            last_use["experts"] = (moe_ring_free, 1)
            for j in range(len(second)):
                load_chunk(sp, AT_SECOND + j)
            sp.wait_ge(stage_done, 3 * N_STAGES)
            sp.dma_start(out, X[:, :, 0:T]).then_inc(out_done, 16)
            sp.wait_ge(out_done, 16)



def kernel(**inputs):
    from concourse import bacc
    from concourse.bass_utils import run_bass_kernel_spmd

    arrays = layout(inputs)
    nc = bacc.Bacc("TRN2", target_bir_lowering=False, num_devices=1, dynamic_dma_scratch_size=1024)
    d = {n: nc.dram_tensor(f"in_{n}", a.shape, mybir.dt.from_np(a.dtype), kind="ExternalInput").ap() for n, a in arrays.items()}
    out = nc.dram_tensor("out_xT", (P, DT, T), F32, kind="ExternalOutput").ap()
    build(nc, d, out)
    r = run_bass_kernel_spmd(nc, [{f"in_{n}": a for n, a in arrays.items()}], core_ids=[0])
    got = r.results[0]["out_xT"]
    return np.ascontiguousarray(got.transpose(2, 1, 0).reshape(1, T, D))
```
